# Optimizing a Trainium2 kernel written in Bass

```python
import math
import jax, jax.numpy as jnp
from jax import lax
import numpy as np

D_MODEL = 1024
BATCH = 1
SEQ = 512
DEPTH = 1

RWKV_HEADS = 8
RWKV_HEAD = 64
RWKV_W = RWKV_HEADS * RWKV_HEAD
DIFF_HEADS = 4
DIFF_QK = 64
DIFF_V = 2 * DIFF_QK
DIFF_W = DIFF_HEADS * DIFF_V
MIX_W = RWKV_W + DIFF_W
DECAY_LORA = 64
ICLR_LORA = 64
GATE_LORA = 160
RWKV_COLS = [RWKV_W, RWKV_W, RWKV_W, DECAY_LORA, ICLR_LORA, GATE_LORA]
SHIFT_COLS = sum(RWKV_COLS)
DIFF_COLS = [DIFF_HEADS * 2 * DIFF_QK, DIFF_HEADS * 2 * DIFF_QK, DIFF_W]
PROJ_W = SHIFT_COLS + sum(DIFF_COLS)
D_FF = 2816
FFN_RES = 0.5
Q_BLOCK = 128
NORM_EPS = 1e-6
GN_EPS = 64e-5
SUBLN_EPS = 1e-5


def _split(t, widths):
    idx = [int(v) for v in np.cumsum(widths)[:-1]]
    return jnp.split(t, idx, axis=-1)

def rmsnorm(x, g, eps=NORM_EPS):
    xf = x.astype(jnp.float32)
    y = xf * lax.rsqrt(jnp.mean(xf * xf, axis=-1, keepdims=True) + eps)
    return (y * g.astype(jnp.float32)).astype(x.dtype)

def swiglu(x, w_gate, w_up, w_down):
    return (jax.nn.silu(x @ w_gate) * (x @ w_up)) @ w_down

def token_shift(p):
    return jnp.pad(p, ((0, 0), (1, 0), (0, 0)))[:, :-1]

def rwkv7_scan(r, w, k, v, a, b):
    B, T, H, N = r.shape

    def step(S, inp):
        r_t, w_t, k_t, v_t, a_t, b_t = inp
        sa = jnp.einsum('bhij,bhj->bhi', S, a_t)
        S = (S * w_t[:, :, None, :] + sa[..., None] * b_t[:, :, None, :]
             + v_t[..., None] * k_t[:, :, None, :])
        y = jnp.einsum('bhij,bhj->bhi', S, r_t)
        return S, y

    S0 = jnp.zeros((B, H, N, N), jnp.float32)
    xs = tuple(jnp.moveaxis(t, 1, 0) for t in (r, w, k, v, a, b))
    _, ys = lax.scan(step, S0, xs)
    return jnp.moveaxis(ys, 0, 1)

def rwkv7_group(p_r, p_k, p_v, p_wd, p_ad, p_gd, w0, w_up, a0, a_up, g_up,
                k_k, k_a, r_k, gn_w, gn_b):
    B, T, _ = p_r.shape
    H, N = RWKV_HEADS, RWKV_HEAD
    f32 = jnp.float32
    logw = -jax.nn.softplus(-(w0 + jnp.tanh(p_wd) @ w_up)) - 0.5
    decay = jnp.exp(-jnp.exp(logw.astype(f32)))
    iclr = jax.nn.sigmoid(a0 + p_ad @ a_up)
    gate = jax.nn.sigmoid(p_gd) @ g_up
    kk = (p_k * k_k).reshape(B, T, H, N).astype(f32)
    kk = kk * lax.rsqrt(jnp.maximum(jnp.sum(kk * kk, -1, keepdims=True), 1e-24))
    k = p_k * (1.0 + (iclr - 1.0) * k_a)
    hs = lambda t: t.reshape(B, T, H, N).astype(f32)
    r_h, k_h, v_h, a_h = hs(p_r), hs(k), hs(p_v), hs(iclr)
    y = rwkv7_scan(r_h, hs(decay), k_h, v_h, -kk, kk * a_h)
    mu = jnp.mean(y, -1, keepdims=True)
    var = jnp.mean(jnp.square(y - mu), -1, keepdims=True)
    y = (y - mu) * lax.rsqrt(var + GN_EPS)
    y = y * gn_w.reshape(H, N).astype(f32) + gn_b.reshape(H, N).astype(f32)
    y = y + jnp.sum(r_h * k_h * r_k.astype(f32), -1, keepdims=True) * v_h
    y = y.reshape(B, T, RWKV_W)
    return (y * gate.astype(f32)).astype(p_r.dtype)

def diff_attention_group(q, k, v, lam_q1, lam_k1, lam_q2, lam_k2, subln_w, lambda_init):
    B, T, _ = q.shape
    H, D = DIFF_HEADS, DIFF_QK
    f32 = jnp.float32
    nb = T // Q_BLOCK
    qh = q.reshape(B, nb, Q_BLOCK, H, 2, D).transpose(1, 0, 2, 3, 4, 5).astype(f32)
    kh = k.reshape(B, T, H, 2, D).astype(f32)
    vh = v.reshape(B, T, H, DIFF_V).astype(f32)
    lam = (jnp.exp(jnp.sum(lam_q1.astype(f32) * lam_k1.astype(f32)))
           - jnp.exp(jnp.sum(lam_q2.astype(f32) * lam_k2.astype(f32))) + lambda_init)
    scale = D ** -0.5
    key_pos = jnp.arange(T)

    def block(args):
        qi, i = args
        s = jnp.einsum('bqhcd,bkhcd->bhcqk', qi, kh) * scale
        q_pos = i * Q_BLOCK + jnp.arange(Q_BLOCK)
        mask = key_pos[None, :] <= q_pos[:, None]
        s = jnp.where(mask, s, -jnp.inf)
        p = jax.nn.softmax(s, axis=-1)
        pd = p[:, :, 0] - lam * p[:, :, 1]
        return jnp.einsum('bhqk,bkhe->bqhe', pd, vh)

    o = lax.map(block, (qh, jnp.arange(nb)))
    o = jnp.moveaxis(o, 0, 1).reshape(B, T, H, DIFF_V)
    o = o * lax.rsqrt(jnp.mean(o * o, -1, keepdims=True) + SUBLN_EPS) * subln_w.astype(f32)
    o = o * (1.0 - lambda_init)
    return o.reshape(B, T, DIFF_W).astype(q.dtype)

def first_inputs(seed: int = 0) -> dict:
    key = jax.random.key(seed)
    ks = iter(jax.random.split(key, 48))
    L, D, F = DEPTH, D_MODEL, D_FF
    nrm = lambda shape, s: jax.random.normal(next(ks), shape, jnp.float32) * s
    gain = lambda shape: 1.0 + nrm(shape, 0.02)
    n = jnp.arange(RWKV_W, dtype=jnp.float32) / (RWKV_W - 1)
    decay_speed = -7.0 + 5.0 * n ** 0.85 + 0.5
    return {
        "x": jax.random.normal(next(ks), (BATCH, SEQ, D), jnp.float32),
        "ffn1_pre_g": gain((L, D)),
        "ffn1_post_g": gain((L, D)),
        "ffn1_w_gate": nrm((L, D, F), D ** -0.5),
        "ffn1_w_up": nrm((L, D, F), D ** -0.5),
        "ffn1_w_down": nrm((L, F, D), F ** -0.5),
        "mix_pre_g": gain((L, D)),
        "mix_post_g": gain((L, D)),
        "w_in": nrm((L, D, PROJ_W), D ** -0.5),
        "shift_mu": jax.random.uniform(next(ks), (L, SHIFT_COLS), jnp.float32),
        "w_o": nrm((L, MIX_W, D), MIX_W ** -0.5),
        "rwkv_w0": decay_speed[None, :] + nrm((L, RWKV_W), 0.1),
        "rwkv_w_up": nrm((L, DECAY_LORA, RWKV_W), 0.5 * DECAY_LORA ** -0.5),
        "rwkv_a0": nrm((L, RWKV_W), 0.1),
        "rwkv_a_up": nrm((L, ICLR_LORA, RWKV_W), 0.5 * ICLR_LORA ** -0.5),
        "rwkv_g_up": nrm((L, GATE_LORA, RWKV_W), GATE_LORA ** -0.5),
        "rwkv_k_k": 0.85 + nrm((L, RWKV_W), 0.02),
        "rwkv_k_a": gain((L, RWKV_W)),
        "rwkv_r_k": nrm((L, RWKV_HEADS, RWKV_HEAD), 0.1),
        "rwkv_gn_w": gain((L, RWKV_W)),
        "rwkv_gn_b": nrm((L, RWKV_W), 0.02),
        "diff_lam_q1": nrm((L, DIFF_QK), 0.1),
        "diff_lam_k1": nrm((L, DIFF_QK), 0.1),
        "diff_lam_q2": nrm((L, DIFF_QK), 0.1),
        "diff_lam_k2": nrm((L, DIFF_QK), 0.1),
        "diff_subln_w": gain((L, DIFF_V)),
        "ffn2_pre_g": gain((L, D)),
        "ffn2_post_g": gain((L, D)),
        "ffn2_w_gate": nrm((L, D, F), D ** -0.5),
        "ffn2_w_up": nrm((L, D, F), D ** -0.5),
        "ffn2_w_down": nrm((L, F, D), F ** -0.5),
    }

def first_block(x, ffn1_pre_g, ffn1_post_g, ffn1_w_gate, ffn1_w_up, ffn1_w_down,
              mix_pre_g, mix_post_g, w_in, shift_mu, w_o,
              rwkv_w0, rwkv_w_up, rwkv_a0, rwkv_a_up, rwkv_g_up, rwkv_k_k, rwkv_k_a,
              rwkv_r_k, rwkv_gn_w, rwkv_gn_b,
              diff_lam_q1, diff_lam_k1, diff_lam_q2, diff_lam_k2, diff_subln_w,
              ffn2_pre_g, ffn2_post_g, ffn2_w_gate, ffn2_w_up, ffn2_w_down):
    for l in range(DEPTH):
        lambda_init = 0.8 - 0.6 * math.exp(-0.3 * l)
        h = rmsnorm(x, ffn1_pre_g[l])
        x = x + FFN_RES * rmsnorm(swiglu(h, ffn1_w_gate[l], ffn1_w_up[l], ffn1_w_down[l]), ffn1_post_g[l])
        h = rmsnorm(x, mix_pre_g[l])
        p = h @ w_in[l]
        p_rw, p_diff = p[..., :SHIFT_COLS], p[..., SHIFT_COLS:]
        p_rw = p_rw + (token_shift(p_rw) - p_rw) * shift_mu[l]
        p_r, p_k, p_v, p_wd, p_ad, p_gd = _split(p_rw, RWKV_COLS)
        q_d, k_d, v_d = _split(p_diff, DIFF_COLS)
        y_rwkv = rwkv7_group(p_r, p_k, p_v, p_wd, p_ad, p_gd,
                             rwkv_w0[l], rwkv_w_up[l], rwkv_a0[l], rwkv_a_up[l], rwkv_g_up[l],
                             rwkv_k_k[l], rwkv_k_a[l], rwkv_r_k[l], rwkv_gn_w[l], rwkv_gn_b[l])
        y_diff = diff_attention_group(q_d, k_d, v_d, diff_lam_q1[l], diff_lam_k1[l],
                                      diff_lam_q2[l], diff_lam_k2[l], diff_subln_w[l], lambda_init)
        y = jnp.concatenate([y_rwkv, y_diff], axis=-1) @ w_o[l]
        x = x + rmsnorm(y, mix_post_g[l])
        h = rmsnorm(x, ffn2_pre_g[l])
        x = x + FFN_RES * rmsnorm(swiglu(h, ffn2_w_gate[l], ffn2_w_up[l], ffn2_w_down[l]), ffn2_post_g[l])
    return x


_first_inputs = first_inputs


def first_inputs(seed=0):
    import zlib

    import numpy as np

    out = dict(_first_inputs(seed))
    spreads = {}
    factors = {'ffn1_pre_g': 2.784,
     'ffn1_post_g': 4.22,
     'mix_post_g': 11.227,
     'rwkv_w_up': 4.336,
     'rwkv_a0': 3.307,
     'rwkv_k_k': 44.497,
     'rwkv_k_a': 17.825,
     'rwkv_gn_w': 31.38,
     'rwkv_gn_b': 31.197,
     'diff_lam_q1': 3.343,
     'diff_lam_k1': 5.583,
     'diff_subln_w': 21.423,
     'ffn2_pre_g': 18.874,
     'ffn2_post_g': 38.538}
    for name, (base, spread) in spreads.items():
        noise = np.random.default_rng([zlib.crc32(name.encode()), seed]).standard_normal(out[name].shape)
        drawn = base * np.exp(spread * noise) if base else spread * noise
        out[name] = __import__('jax').numpy.asarray(drawn.astype(out[name].dtype))
    for name, factor in factors.items():
        out[name] = (out[name] * factor).astype(out[name].dtype)
    return out


_narrow_inputs = first_inputs


def first_inputs(seed=0):

    out = dict(_narrow_inputs(seed))
    wider = {'rwkv_k_k': 4.97,
     'rwkv_k_a': 3.03,
     'rwkv_gn_w': 3.69,
     'rwkv_gn_b': 3.69,
     'diff_subln_w': 3.69,
     'ffn2_post_g': 4.08}
    for name, times in wider.items():
        mean = out[name].mean()
        out[name] = (mean + times * (out[name] - mean)).astype(out[name].dtype)
    return out


DEPTH_2 = 2

N_A_LAYERS = DEPTH_2 // 2
N_B_LAYERS = DEPTH_2 - N_A_LAYERS

EXPAND = 2
D_A = EXPAND * D_MODEL
POOL_WINDOWS = (2, 4, 8, 16)
N_POOL_GROUPS = len(POOL_WINDOWS)
POOL_GW = D_A // N_POOL_GROUPS

ATTN_PAIRS = ((128, 1), (512, 4), (2048, 16))
N_GROUPS = len(ATTN_PAIRS)
N_HEADS = 16
HEAD_DIM = D_MODEL // N_HEADS
D_B = N_HEADS * HEAD_DIM
BLK = 128

DN_ALPHA = (2 * DEPTH_2) ** 0.25
DN_BETA = (8 * DEPTH_2) ** -0.25
LN_EPS = 1e-5
NEG_INF = -1e30


def layer_norm(x, g, b):
    xf = x.astype(jnp.float32)
    mu = jnp.mean(xf, axis=-1, keepdims=True)
    var = jnp.mean(jnp.square(xf - mu), axis=-1, keepdims=True)
    y = (xf - mu) * lax.rsqrt(var + LN_EPS) * g.astype(jnp.float32) + b.astype(jnp.float32)
    return y.astype(x.dtype)

def alibi_slopes():
    n = N_GROUPS * N_HEADS
    i = jnp.arange(1, n + 1, dtype=jnp.float32)
    return (2.0 ** (-8.0 * i / n)).reshape(N_GROUPS, N_HEADS)

def pool_mixer(h, w_in, w_grp, scale, w_out):
    B, S, _ = h.shape
    proj = h @ w_in
    u, gate = proj[..., :D_A], proj[..., D_A:]
    uf = u.astype(jnp.float32).reshape(B, S, N_POOL_GROUPS, POOL_GW)
    pos = jnp.arange(S)
    pooled = []
    for g, w in enumerate(POOL_WINDOWS):
        ug = uf[:, :, g]
        cs = jnp.cumsum(ug, axis=1)
        shifted = jnp.pad(cs, ((0, 0), (w, 0), (0, 0)))[:, :S]
        cnt = jnp.minimum(pos + 1, w).astype(jnp.float32)
        pooled.append((cs - shifted) / cnt[None, :, None] - ug)
    pooled = jnp.stack(pooled, axis=2)
    mixed = jnp.einsum('bsgc,gce->bsge', pooled, w_grp.astype(jnp.float32))
    mixed = (mixed.reshape(B, S, D_A) * scale.astype(jnp.float32)).astype(h.dtype)
    return (mixed * jax.nn.silu(gate)) @ w_out

def dilated_window_attention(q, k, v, window, dilation, slopes):
    B, S, H, dh = q.shape
    L = S // dilation
    nblk = -(-L // BLK)
    Lp = nblk * BLK
    win_sub = window // dilation

    def to_sub(t):
        t = t.reshape(B, L, dilation, H, dh)
        t = jnp.pad(t, ((0, 0), (0, Lp - L), (0, 0), (0, 0), (0, 0)))
        return t.reshape(B, nblk, BLK, dilation, H, dh)

    qb, kb, vb = to_sub(q), to_sub(k), to_sub(v)

    def with_prev(t):
        prev = jnp.concatenate([jnp.zeros_like(t[:, :1]), t[:, :-1]], axis=1)
        return jnp.concatenate([prev, t], axis=2)

    kk, vv = with_prev(kb), with_prev(vb)
    scores = jnp.einsum('bnqrhd,bnkrhd->bnrhqk', qb, kk) * (HEAD_DIM ** -0.5)

    a = jnp.arange(BLK)[:, None]
    c = jnp.arange(2 * BLK)[None, :]
    rel = BLK + a - c
    key_pos = (jnp.arange(nblk)[:, None, None] - 1) * BLK + c[None]
    valid = (rel >= 0)[None] & (rel <= win_sub)[None] & (key_pos >= 0)
    bias = -slopes[:, None, None] * (dilation * rel).astype(jnp.float32)[None]
    scores = jnp.where(valid[None, :, None, None], scores + bias[None, None, None], NEG_INF)

    lse = jax.nn.logsumexp(scores, axis=-1)
    p = jnp.exp(scores - lse[..., None])
    out = jnp.einsum('bnrhqk,bnkrhd->bnqrhd', p, vv)
    out = out.reshape(B, Lp, dilation, H, dh)[:, :L].reshape(B, S, H, dh)
    lse = jnp.transpose(lse, (0, 1, 4, 2, 3)).reshape(B, Lp, dilation, H)[:, :L].reshape(B, S, H)
    return out, lse

def dilated_mixer(h, w_in, w_out, k_sh, v_sh, slopes):
    B, S, _ = h.shape
    proj = h @ w_in
    q_all = proj[..., :N_GROUPS * D_B].astype(jnp.float32).reshape(B, S, N_GROUPS, N_HEADS, HEAD_DIM)
    gate = proj[..., N_GROUPS * D_B:]
    kf = k_sh.astype(jnp.float32)
    vf = v_sh.astype(jnp.float32)
    outs, lses = [], []
    for g, (window, dilation) in enumerate(ATTN_PAIRS):
        o, l = dilated_window_attention(q_all[:, :, g], kf[:, :, g], vf[:, :, g], window, dilation, slopes[g])
        outs.append(o)
        lses.append(l)
    wts = jax.nn.softmax(jnp.stack(lses, axis=0), axis=0)
    merged = jnp.sum(wts[..., None] * jnp.stack(outs, axis=0), axis=0)
    merged = merged.reshape(B, S, D_B).astype(h.dtype)
    return (merged * jax.nn.silu(gate)) @ w_out

def second_inputs(seed: int = 0) -> dict:
    key = jax.random.key(seed)
    ks = jax.random.split(key, 12)
    f32 = jnp.float32
    x = jax.random.normal(ks[0], (BATCH, SEQ, D_MODEL), f32)
    w_in_a = jax.random.normal(ks[1], (N_A_LAYERS, D_MODEL, 2 * D_A), f32) * D_MODEL ** -0.5
    w_grp_a = jax.random.normal(ks[2], (N_A_LAYERS, N_POOL_GROUPS, POOL_GW, POOL_GW), f32) * POOL_GW ** -0.5
    scale_a = 1.0 + 0.1 * jax.random.normal(ks[3], (N_A_LAYERS, D_A), f32)
    w_out_a = jax.random.normal(ks[4], (N_A_LAYERS, D_A, D_MODEL), f32) * (D_A ** -0.5) * DN_BETA
    w_kv = jax.random.normal(ks[5], (D_MODEL, 2 * N_GROUPS * D_B), f32) * D_MODEL ** -0.5
    w_in_b = jax.random.normal(ks[6], (N_B_LAYERS, D_MODEL, (N_GROUPS + 1) * D_B), f32) * D_MODEL ** -0.5
    w_out_b = jax.random.normal(ks[7], (N_B_LAYERS, D_B, D_MODEL), f32) * (D_B ** -0.5) * DN_BETA
    ln_g = 1.0 + 0.02 * jax.random.normal(ks[8], (DEPTH_2, D_MODEL), f32)
    ln_b = 0.02 * jax.random.normal(ks[9], (DEPTH_2, D_MODEL), f32)
    return {"x": x, "w_in_a": w_in_a, "w_grp_a": w_grp_a, "scale_a": scale_a, "w_out_a": w_out_a,
            "w_kv": w_kv, "w_in_b": w_in_b, "w_out_b": w_out_b, "ln_g": ln_g, "ln_b": ln_b}

def second_block(x, w_in_a, w_grp_a, scale_a, w_out_a, w_kv, w_in_b, w_out_b, ln_g, ln_b):
    B, S, _ = x.shape
    slopes = alibi_slopes()
    h = x
    k_sh = None
    v_sh = None
    for l in range(DEPTH_2):
        if l < N_A_LAYERS:
            y = pool_mixer(h, w_in_a[l], w_grp_a[l], scale_a[l], w_out_a[l])
        else:
            j = l - N_A_LAYERS
            y = dilated_mixer(h, w_in_b[j], w_out_b[j], k_sh, v_sh, slopes)
        h = layer_norm(DN_ALPHA * h + y, ln_g[l], ln_b[l])
        if l == N_A_LAYERS - 1:
            kv = h @ w_kv
            k_sh = kv[..., :N_GROUPS * D_B].reshape(B, S, N_GROUPS, N_HEADS, HEAD_DIM)
            v_sh = kv[..., N_GROUPS * D_B:].reshape(B, S, N_GROUPS, N_HEADS, HEAD_DIM)
    return h


M_HEADS = 4
M_DV = 128
M_DQK = 64
M_CHUNK = 64
M_CONV = 4
A_HEADS = 8
A_DH = 64
IDX_HEADS = 8
IDX_DIM = 64
TOPK_MAX = 256
REL_BUCKETS = 32
REL_MAX_DIST = 128
FFN_CONV = 3
EPS = 1e-6

M_WIDTH = M_HEADS * M_DV
A_WIDTH = A_HEADS * A_DH
D_MIX = M_WIDTH + A_WIDTH
IN_SIZES = (M_HEADS * M_DQK, M_HEADS * M_DQK, M_WIDTH, M_WIDTH, M_HEADS, M_HEADS,
            A_WIDTH, A_WIDTH, A_WIDTH, IDX_HEADS * IDX_DIM, IDX_DIM, IDX_HEADS)
D_IN = 2 * M_HEADS * M_DQK + 2 * M_WIDTH + 2 * M_HEADS + 3 * A_WIDTH + IDX_HEADS * IDX_DIM + IDX_DIM + IDX_HEADS


def rms_norm(x, g):
    xf = x.astype(jnp.float32)
    y = xf * lax.rsqrt(jnp.mean(xf * xf, axis=-1, keepdims=True) + EPS)
    return (y * g.astype(jnp.float32)).astype(x.dtype)

def causal_dwconv(x, w, b):
    width = w.shape[0]
    s = x.shape[1]
    xp = jnp.pad(x, ((0, 0), (width - 1, 0), (0, 0)))
    y = b + xp[:, 0:s] * w[0]
    for j in range(1, width):
        y = y + xp[:, j:j + s] * w[j]
    return y

def split_cols(z, sizes):
    out, off = [], 0
    for sz in sizes:
        out.append(z[..., off:off + sz])
        off += sz
    return out

def rel_bucket(dist):
    max_exact = REL_BUCKETS // 2
    d = jnp.maximum(dist, 0)
    large = max_exact + (jnp.log(jnp.maximum(d, 1).astype(jnp.float32) / max_exact)
                         / math.log(REL_MAX_DIST / max_exact) * (REL_BUCKETS - max_exact)).astype(jnp.int32)
    large = jnp.minimum(large, REL_BUCKETS - 1)
    return jnp.where(d < max_exact, d, large)

def mlstm_chunkwise(q, k, v, i_pre, f_pre):
    bsz, s, nh, dqk = q.shape
    dv = v.shape[-1]
    L = M_CHUNK
    nc = s // L
    f32 = jnp.float32

    def heads_chunks(t):
        return t.astype(f32).reshape(bsz, nc, L, nh, t.shape[-1]).transpose(0, 3, 1, 2, 4)

    q = heads_chunks(q) * (dqk ** -0.5)
    k = heads_chunks(k)
    v = heads_chunks(v)
    ig = i_pre.astype(f32).reshape(bsz, nc, L, nh).transpose(0, 3, 1, 2)
    logf = jax.nn.log_sigmoid(f_pre.astype(f32)).reshape(bsz, nc, L, nh).transpose(0, 3, 1, 2)

    b = jnp.cumsum(logf, axis=-1)
    g = b[..., -1]
    a = g[..., None] - b + ig
    m_loc = jnp.max(a, axis=-1)
    wgt = jnp.exp(a - m_loc[..., None])
    kv_c = jnp.einsum('bhcl,bhcld,bhcle->bhcde', wgt, k, v)
    ks_c = jnp.einsum('bhcl,bhcld->bhcd', wgt, k)

    def step(carry, xs):
        c_st, n_st, m_st = carry
        kv, ks, gc, ml = xs
        m_new = jnp.maximum(gc + m_st, ml)
        decay = jnp.exp(gc + m_st - m_new)
        scale = jnp.exp(ml - m_new)
        c_new = decay[..., None, None] * c_st + scale[..., None, None] * kv
        n_new = decay[..., None] * n_st + scale[..., None] * ks
        return (c_new, n_new, m_new), (c_st, n_st, m_st)

    init = (jnp.zeros((bsz, nh, dqk, dv), f32), jnp.zeros((bsz, nh, dqk), f32), jnp.zeros((bsz, nh), f32))
    xs = (jnp.moveaxis(kv_c, 2, 0), jnp.moveaxis(ks_c, 2, 0), jnp.moveaxis(g, 2, 0), jnp.moveaxis(m_loc, 2, 0))
    _, (c_prev, n_prev, m_prev) = lax.scan(step, init, xs)
    c_prev = jnp.moveaxis(c_prev, 0, 2)
    n_prev = jnp.moveaxis(n_prev, 0, 2)
    m_prev = jnp.moveaxis(m_prev, 0, 2)

    tril = jnp.tril(jnp.ones((L, L), dtype=bool))
    dmat = b[..., :, None] - b[..., None, :] + ig[..., None, :]
    dmat = jnp.where(tril, dmat, -jnp.inf)
    inter_log = b + m_prev[..., None]
    m_t = jnp.maximum(inter_log, jnp.max(dmat, axis=-1))
    sc = jnp.einsum('bhcld,bhcsd->bhcls', q, k) * jnp.exp(dmat - m_t[..., None])
    inter_w = jnp.exp(inter_log - m_t)
    num = inter_w[..., None] * jnp.einsum('bhcld,bhcde->bhcle', q, c_prev) + jnp.einsum('bhcls,bhcse->bhcle', sc, v)
    den = inter_w * jnp.einsum('bhcld,bhcd->bhcl', q, n_prev) + jnp.sum(sc, axis=-1)
    h = num / jnp.maximum(jnp.abs(den), jnp.exp(-m_t))[..., None]
    return h.transpose(0, 2, 3, 1, 4).reshape(bsz, s, nh, dv)

def dsa_attention(q_att, k_att, v_att, q_idx, k_idx, w_idx, rel_bias):
    bsz, s = q_att.shape[0], q_att.shape[1]
    topk = min(TOPK_MAX, s // 4)
    nqb = s // Q_BLOCK
    key_pos = jnp.arange(s, dtype=jnp.int32)

    def to_blocks(t):
        return t.reshape(bsz, nqb, Q_BLOCK, *t.shape[2:]).swapaxes(0, 1)

    def one_block(args):
        qa, qi, wi, st = args
        qpos = st + jnp.arange(Q_BLOCK, dtype=jnp.int32)
        isc = jnp.einsum('bqhd,bsd->bqhs', qi, k_idx).astype(jnp.float32) * (IDX_DIM ** -0.5)
        score = jnp.einsum('bqhs,bqh->bqs', jax.nn.relu(isc), wi.astype(jnp.float32))
        score = jnp.where(key_pos[None, None, :] <= qpos[None, :, None], score, -jnp.inf)
        _, idx = lax.top_k(score, topk)
        valid = idx <= qpos[None, :, None]
        ks = jax.vmap(lambda kb, ib: kb[ib])(k_att, idx)
        vs = jax.vmap(lambda vb, ib: vb[ib])(v_att, idx)
        bias = rel_bias[rel_bucket(qpos[None, :, None] - idx)]
        logits = jnp.einsum('bqhd,bqkhd->bqhk', qa, ks).astype(jnp.float32) * (A_DH ** -0.5)
        logits = logits + bias.astype(jnp.float32).transpose(0, 1, 3, 2)
        logits = jnp.where(valid[:, :, None, :], logits, -jnp.inf)
        p = jax.nn.softmax(logits, axis=-1)
        return jnp.einsum('bqhk,bqkhd->bqhd', p.astype(vs.dtype), vs)

    starts = jnp.arange(nqb, dtype=jnp.int32) * Q_BLOCK
    out = lax.map(one_block, (to_blocks(q_att), to_blocks(q_idx), to_blocks(w_idx), starts))
    return out.swapaxes(0, 1).reshape(bsz, s, A_HEADS, A_DH)

def third_inputs(seed: int = 0) -> dict:
    key = jax.random.key(seed)
    ks = jax.random.split(key, 20)
    f32 = jnp.float32
    nrm = lambda k, shape, scale: jax.random.normal(k, shape, f32) * scale
    return {
        'x': nrm(ks[0], (BATCH, SEQ, D_MODEL), 1.0),
        'norm_mix': 1.0 + nrm(ks[1], (DEPTH, D_MODEL), 0.01),
        'w_in': nrm(ks[2], (DEPTH, D_MODEL, D_IN), D_MODEL ** -0.5),
        'mlstm_conv_w': nrm(ks[3], (DEPTH, M_CONV, 2 * M_HEADS * M_DQK), M_CONV ** -0.5),
        'mlstm_conv_b': nrm(ks[4], (DEPTH, 2 * M_HEADS * M_DQK), 0.01),
        'i_bias': nrm(ks[5], (DEPTH, M_HEADS), 0.1),
        'f_bias': 3.0 + nrm(ks[6], (DEPTH, M_HEADS), 0.5),
        'mlstm_norm': 1.0 + nrm(ks[7], (DEPTH, M_WIDTH), 0.01),
        'idx_k_norm': 1.0 + nrm(ks[8], (DEPTH, IDX_DIM), 0.01),
        'rel_bias': nrm(ks[9], (REL_BUCKETS, A_HEADS), 0.5),
        'w_out': nrm(ks[10], (DEPTH, D_MIX, D_MODEL), D_MIX ** -0.5),
        'norm_ffn': 1.0 + nrm(ks[11], (DEPTH, D_MODEL), 0.01),
        'w_up': nrm(ks[12], (DEPTH, D_MODEL, 2 * D_FF), D_MODEL ** -0.5),
        'ffn_conv_w': nrm(ks[13], (DEPTH, FFN_CONV, 2 * D_FF), FFN_CONV ** -0.5),
        'ffn_conv_b': nrm(ks[14], (DEPTH, 2 * D_FF), 0.01),
        'w_down': nrm(ks[15], (DEPTH, D_FF, D_MODEL), D_FF ** -0.5),
        'norm_final': 1.0 + nrm(ks[16], (D_MODEL,), 0.01),
    }

def third_block(x, norm_mix, w_in, mlstm_conv_w, mlstm_conv_b, i_bias, f_bias, mlstm_norm,
              idx_k_norm, rel_bias, w_out, norm_ffn, w_up, ffn_conv_w, ffn_conv_b, w_down, norm_final):
    bsz, s, _ = x.shape
    for l in range(DEPTH):
        h = rms_norm(x, norm_mix[l])
        z = h @ w_in[l]
        (m_q, m_k, m_v, m_o, m_i, m_f, a_q, a_k, a_v, i_q, i_k, i_w) = split_cols(z, IN_SIZES)

        qk = jax.nn.silu(causal_dwconv(jnp.concatenate([m_q, m_k], axis=-1), mlstm_conv_w[l], mlstm_conv_b[l]))
        m_q, m_k = qk[..., :M_HEADS * M_DQK], qk[..., M_HEADS * M_DQK:]
        hm = mlstm_chunkwise(m_q.reshape(bsz, s, M_HEADS, M_DQK), m_k.reshape(bsz, s, M_HEADS, M_DQK),
                             m_v.reshape(bsz, s, M_HEADS, M_DV), m_i + i_bias[l], m_f + f_bias[l])
        hm = rms_norm(hm, mlstm_norm[l].reshape(M_HEADS, M_DV)).astype(x.dtype)
        hm = jax.nn.sigmoid(m_o) * hm.reshape(bsz, s, M_WIDTH)

        ha = dsa_attention(a_q.reshape(bsz, s, A_HEADS, A_DH), a_k.reshape(bsz, s, A_HEADS, A_DH),
                           a_v.reshape(bsz, s, A_HEADS, A_DH), i_q.reshape(bsz, s, IDX_HEADS, IDX_DIM),
                           rms_norm(i_k, idx_k_norm[l]), i_w * (IDX_HEADS ** -0.5), rel_bias)
        ha = ha.reshape(bsz, s, A_WIDTH)

        x = x + jnp.concatenate([hm, ha], axis=-1) @ w_out[l]

        h = rms_norm(x, norm_ffn[l])
        u = causal_dwconv(h @ w_up[l], ffn_conv_w[l], ffn_conv_b[l])
        gate, val = u[..., :D_FF], u[..., D_FF:]
        x = x + (jax.nn.silu(gate) * val) @ w_down[l]
    return rms_norm(x, norm_final)


_first_inputs_3 = third_inputs


def third_inputs(seed=0):
    import zlib

    import numpy as np

    out = dict(_first_inputs_3(seed))
    spreads = {}
    factors = {'norm_mix': 4.225,
     'mlstm_conv_b': 8.0,
     'i_bias': 8.0,
     'mlstm_norm': 8.0,
     'idx_k_norm': 7.559,
     'norm_ffn': 7.797,
     'ffn_conv_b': 8.0,
     'norm_final': 5.707}
    for name, (base, spread) in spreads.items():
        noise = np.random.default_rng([zlib.crc32(name.encode()), seed]).standard_normal(out[name].shape)
        drawn = base * np.exp(spread * noise) if base else spread * noise
        out[name] = __import__('jax').numpy.asarray(drawn.astype(out[name].dtype))
    for name, factor in factors.items():
        out[name] = (out[name] * factor).astype(out[name].dtype)
    return out


_narrow_inputs_3 = third_inputs


def third_inputs(seed=0):

    out = dict(_narrow_inputs_3(seed))
    wider = {'i_bias': 12.0,
     'mlstm_norm': 5.89,
     'norm_ffn': 4.5,
     'ffn_conv_b': 4.52,
     'norm_final': 6.43}
    for name, times in wider.items():
        mean = out[name].mean()
        out[name] = (mean + times * (out[name] - mean)).astype(out[name].dtype)
    return out


def setup_inputs(seed=0):
    out = dict(first_inputs(seed))
    for name, value in second_inputs(seed + 1).items():
        if name != "x":
            out[name + "_2"] = value
    for name, value in third_inputs(seed + 2).items():
        if name != "x":
            out[name + "_3"] = value
    return out


def reference(
    x, ffn1_pre_g, ffn1_post_g, ffn1_w_gate, ffn1_w_up, ffn1_w_down, mix_pre_g, mix_post_g,
    w_in, shift_mu, w_o, rwkv_w0, rwkv_w_up, rwkv_a0, rwkv_a_up, rwkv_g_up, rwkv_k_k, rwkv_k_a,
    rwkv_r_k, rwkv_gn_w, rwkv_gn_b, diff_lam_q1, diff_lam_k1, diff_lam_q2, diff_lam_k2,
    diff_subln_w, ffn2_pre_g, ffn2_post_g, ffn2_w_gate, ffn2_w_up, ffn2_w_down, w_in_a_2,
    w_grp_a_2, scale_a_2, w_out_a_2, w_kv_2, w_in_b_2, w_out_b_2, ln_g_2, ln_b_2, norm_mix_3,
    w_in_3, mlstm_conv_w_3, mlstm_conv_b_3, i_bias_3, f_bias_3, mlstm_norm_3, idx_k_norm_3,
    rel_bias_3, w_out_3, norm_ffn_3, w_up_3, ffn_conv_w_3, ffn_conv_b_3, w_down_3, norm_final_3,
):
    x = first_block(
        x, ffn1_pre_g, ffn1_post_g, ffn1_w_gate, ffn1_w_up, ffn1_w_down, mix_pre_g, mix_post_g,
        w_in, shift_mu, w_o, rwkv_w0, rwkv_w_up, rwkv_a0, rwkv_a_up, rwkv_g_up, rwkv_k_k,
        rwkv_k_a, rwkv_r_k, rwkv_gn_w, rwkv_gn_b, diff_lam_q1, diff_lam_k1, diff_lam_q2,
        diff_lam_k2, diff_subln_w, ffn2_pre_g, ffn2_post_g, ffn2_w_gate, ffn2_w_up, ffn2_w_down,
    )
    x = second_block(
        x, w_in_a_2, w_grp_a_2, scale_a_2, w_out_a_2, w_kv_2, w_in_b_2, w_out_b_2, ln_g_2,
        ln_b_2,
    )
    return third_block(
        x, norm_mix_3, w_in_3, mlstm_conv_w_3, mlstm_conv_b_3, i_bias_3, f_bias_3, mlstm_norm_3,
        idx_k_norm_3, rel_bias_3, w_out_3, norm_ffn_3, w_up_3, ffn_conv_w_3, ffn_conv_b_3,
        w_down_3, norm_final_3,
    )


_drawn_inputs = setup_inputs


def setup_inputs(seed=0):
    import zlib

    import numpy as np

    out = dict(_drawn_inputs(seed))
    spreads = {}
    factors = {'mlstm_conv_b_3': 8.0}
    for name, (base, spread) in spreads.items():
        noise = np.random.default_rng([zlib.crc32(name.encode()), seed]).standard_normal(out[name].shape)
        drawn = base * np.exp(spread * noise) if base else spread * noise
        out[name] = __import__('jax').numpy.asarray(drawn.astype(out[name].dtype))
    for name, factor in factors.items():
        out[name] = (out[name] * factor).astype(out[name].dtype)
    return out
```

```python
from contextlib import ExitStack, contextmanager
import math

import concourse.bass as bass
from concourse import mybir
from concourse.alu_op_type import AluOpType as ALU
import numpy as np

F32 = mybir.dt.float32
ACT = mybir.ActivationFunctionType
AX = mybir.AxisListType.X

P = 128
T = 512
D = 1024
KT = D // P
TT = T // P
FF = 2816
FT = FF // P
HD = 64
NEG = -1e30
SLOT = 16
LC = 64
NCH = T // LC
LAM0 = 0.8 - 0.6 * math.exp(0.0)
LOG_DECAY = -math.exp(-0.5)
ALPHA = (2 * 2) ** 0.25
GROUPS = ((128, 1), (512, 4), (2048, 16))
TOPK = min(256, T // 4)
TAKEN = -3e38


class Loop:

    def __init__(self, index, trips, adds):
        self.index, self.trips, self.adds, self.reg, self.base = index, trips, adds, None, {}


class Token:

    def __init__(self, sem, n, loops):
        self.sem, self.n, self.loops = sem, n, tuple(loops)


class Count:

    def __init__(self, prog, name, start=None):
        self.prog, self.name, self.n = prog, name, 0
        self.sem = prog.nc.alloc_semaphore(name)
        if start is not None:
            start.sem_inc(self.sem, 1)
            self.n = 1
        prog.counts.append(self)

    def add(self, ins, k=1):
        ins.then_inc(self.sem, k)
        self.n += k
        return self.now()

    def now(self):
        return Token(self, self.n, self.prog.loops)


class Engine:

    def __init__(self, prog, eng, name, chained):
        self.prog, self.eng, self.name, self.chained = prog, eng, name, chained
        self.count = Count(prog, "done_" + name, eng)
        self.last = None
        self.pending = None

    def wait(self, token):
        if token is None:
            return
        value = token.n
        for loop in token.loops:
            step = loop.adds.get(token.sem.name, 0)
            if loop in self.prog.loops:
                if step:
                    value = value + loop.reg * step
            else:
                value = value + (loop.trips - 1) * step
        if isinstance(value, int) and value == 0:
            return
        self.eng.wait_ge(token.sem.sem, value)

    def after(self, *tokens):
        for t in tokens:
            self.wait(t)
        if self.chained:
            self.wait(self.pending)
            self.pending = None
        return self.eng

    def do(self, ins, count=None, k=1):
        self.last = self.pending = (count or self.count).add(ins, k)
        return self.last


class Program:

    def __init__(self, nc, adds_of):
        self.nc, self.adds_of, self.seen = nc, adds_of, []
        self.counts, self.loops = [], []
        self.pe = Engine(self, nc.tensor, "pe", False)
        self.act = Engine(self, nc.scalar, "act", True)
        self.dve = Engine(self, nc.vector, "dve", True)
        self.pool = Engine(self, nc.gpsimd, "pool", True)
        self.sp = Engine(self, nc.sync, "sp", False)
        self.compute = [self.pe, self.act, self.dve, self.pool]
        self.ndma = 0

    @contextmanager
    def loop(self, trips):
        for e in self.compute:
            if e.chained:
                e.after()
        lp = Loop(len(self.seen), trips, self.adds_of.get(len(self.seen), {}))
        self.seen.append(lp)
        lp.base = {c.name: c.n for c in self.counts}
        with self.nc.Fori(0, trips) as reg:
            lp.reg = reg
            self.loops.append(lp)
            yield reg
            for e in self.compute:
                if e.chained:
                    e.after()
            self.loops.pop()
        lp.counted = {c.name: c.n - lp.base.get(c.name, 0) for c in self.counts if c.n != lp.base.get(c.name, 0)}
        for c in self.counts:
            c.n += (trips - 1) * lp.adds.get(c.name, 0)

    def join(self):
        lasts = [(e, e.last) for e in self.compute]
        for e in self.compute:
            for o, last in lasts:
                if (o is not e or e.chained) and last is not None:
                    e.wait(last)
            e.pending = None

    def dma(self, out, in_, after=(), eng=None):
        e = eng or self.sp
        for t in after:
            e.wait(t)
        self.ndma += 1
        c = Count(self, f"moved_{self.ndma}")
        return c.add(e.eng.dma_start(out, in_), 16)


def weight_plan(blocks):
    plan = []

    def tiles(name, cols, kt=KT, row=0):
        return [(name, row + k * P, P, c, w, 0) for c, w in cols for k in range(kt)]

    def pairs(name, c0, n, kt=KT):
        for p in range(n // 2):
            plan.append(tiles(name, [(c0 + (2 * p + j) * P, P) for j in (0, 1)], kt))

    def gated(name_a, a0, name_b, b0, n):
        for p in range(n // 2):
            for name, c0 in ((name_a, a0), (name_b, b0)):
                plan.append(tiles(name, [(c0 + (2 * p + j) * P, P) for j in (0, 1)]))

    def down(name):
        for n in range(KT):
            for half in (0, 1):
                plan.append([(name, (half * FT // 2 + k) * P, P, n * P, P, 0) for k in range(FT // 2)])

    def qkv(name, q, k, v, n):
        for h in range(n):
            plan.append(tiles(name, [(q + h * P, P), (k + h * P, P)]))
            plan.append(tiles(name, [(v + h * P, P)]))

    if 1 in blocks:
        gated("ffn1_w_gate", 0, "ffn1_w_up", 0, FT)
        down("ffn1_w_down")
        qkv("w_in", 1824, 2336, 2848, 4)
        pairs("w_in", 0, 12)
        plan.append(tiles("w_in", [(1536, P), (1664, P)]))
        plan.append(tiles("w_in", [(1792, 32)]))
        plan.append([[("rwkv_w_up", 0, 64, c * P, P, 0), ("rwkv_a_up", 0, 64, c * P, P, 64)] for c in range(4)]
                    + [("rwkv_g_up", 0, P, c * P, P, 0) for c in range(4)]
                    + [("rwkv_g_up", P, 32, c * P, P, 0) for c in range(4)])
        pairs("w_o", 0, KT)
        gated("ffn2_w_gate", 0, "ffn2_w_up", 0, FT)
        down("ffn2_w_down")
    if 2 in blocks:
        for g in range(4):
            pairs("w_in_a_2", g * 512, 4)
            plan.append([("w_grp_a_2", g * 512 + k * P, P, n * P, P, 0) for n in range(4) for k in range(4)])
            pairs("w_in_a_2", 2048 + g * 512, 4)
        for n in range(KT):
            plan.append([("w_out_a_2", k * P, P, n * P, P, 0) for k in range(16)])
        for g in range(3):
            for h in range(8):
                c = g * D + h * P
                plan.append(tiles("w_in_b_2", [(c, P)]) + tiles("w_kv_2", [(c, P)]))
                plan.append(tiles("w_kv_2", [(3 * D + c, P)]))
        pairs("w_in_b_2", 3 * D, 8)
        pairs("w_out_b_2", 0, KT)
    if 3 in blocks:
        pairs("w_in_3", 0, 4)
        pairs("w_in_3", 512, 8)
        plan.append(tiles("w_in_3", [(1536, 8), (3656, 8)]))
        plan.append([[("w_in_3", k * P, P, 3592, 64, 0), ("w_in_3", k * P, P, 3592, 64, 0, 64)]
                     for k in range(KT)])
        pairs("w_in_3", 3080, 4)
        qkv("w_in_3", 1544, 2056, 2568, 4)
        pairs("w_out_3", 0, KT)
        gated("w_up_3", 0, "w_up_3", FF, FT)
        down("w_down_3")
    return plan


def column_plan():
    want = [("ffn1_pre_g", 8), ("ffn1_post_g", 8), ("mix_pre_g", 8), ("mix_post_g", 8), ("shift_mu", 15),
            ("rwkv_w0", 4), ("rwkv_a0", 4), ("rwkv_k_k", 4), ("rwkv_k_a", 4), ("rwkv_r_k", 4), ("rwkv_gn_w", 4),
            ("rwkv_gn_b", 4), ("diff_lam_q1", 1), ("diff_lam_q2", 1), ("diff_lam_k1", 1), ("diff_lam_k2", 1),
            ("diff_subln_w", 1), ("ffn2_pre_g", 8), ("ffn2_post_g", 8), ("scale_a_2", 16), ("ln_g_2", 16),
            ("ln_b_2", 16), ("norm_mix_3", 8), ("mlstm_conv_w_3", 16), ("mlstm_conv_b_3", 4), ("i_bias_3", 1),
            ("f_bias_3", 1), ("mlstm_norm_3", 4), ("idx_k_norm_3", 1), ("norm_ffn_3", 8),
            ("ffn_conv_w_3", 132), ("ffn_conv_b_3", 44), ("norm_final_3", 8)]
    at, n = {}, 0
    for name, k in want:
        at[name] = n
        n += k
    return at, n, want


def permuted(tokens):
    return tokens.rearrange("p (m a r) -> p r a m", m=T // 16, a=4, r=4)


def constants():
    i = np.arange(P)
    c = {}
    c["ident"] = np.eye(P)
    c["ones"] = np.ones((P, P))
    c["headones"] = (i[:, None] // HD == i[None] // HD) * 1.0
    c["causal"] = np.where(i[None] <= i[:, None], 0.0, NEG)
    c["causal_t"] = np.where(i[:, None] <= i[None], 0.0, NEG)
    s, t = i[:, None] % LC, i[None] % LC
    c["pairmask"] = np.where(i[None] < LC, s < t, s <= t) * 1.0
    j = np.arange(LC)
    up, blk = j[:, None] < j[None], j[:, None] // 16 == j[None] // 16
    for name, m in (("near", up & blk), ("far", up & ~blk), ("near_t", up.T & blk)):
        z = np.zeros((P, LC))
        z[:LC] = m
        c[name] = z
    z = np.zeros((P, LC))
    z[:LC] = np.eye(LC)
    c["ident64"] = z
    c["reset"] = np.broadcast_to((np.arange(T) % LC != 0) * 1.0, (P, T))
    rel = P + i[:, None] - np.arange(2 * P)[None]
    c["dist0a"] = np.where(np.arange(2 * P)[None] < P, 1e30, np.where(rel >= 0, rel, 1e30))
    c["dist0"] = np.where((rel >= 0) & (rel <= GROUPS[0][0]), rel, 1e30)
    d = i[:, None] - i[None]
    tok = lambda q: 4 * (4 * (q % 32) + q // 32)
    dt = tok(i)[:, None] - tok(i)[None]
    c["dist1"] = np.where(dt >= 0, dt, 1e30)
    c["dist2"] = np.where((dt >= 0) & (i[:, None] // 32 == i[None] // 32), dt, 1e30)
    k = np.arange(1, 49, dtype=np.float32)
    sl = np.float32(2.0) ** (np.float32(-8.0) * k / np.float32(48))
    c["slopes"] = np.broadcast_to(-sl, (P, 48))
    c["early"] = np.broadcast_to(np.concatenate([w / np.minimum(np.arange(16) + 1, w) / w for w in (2, 4, 8, 16)]), (P, 64))
    z = np.zeros((P, 4 * P))
    for h in range(4):
        z[h, h * P:(h + 1) * P] = 1
    c["pick"] = z
    dist = np.maximum(T - 1 - np.arange(640), 0)
    large = 16 + np.floor(np.log(np.maximum(dist, 1) / 16.0) / math.log(8.0) * 16 + 1e-9).astype(int)
    bucket = np.where(dist < 16, dist, np.minimum(large, 31))
    c["anti"] = np.eye(P)[::-1]
    z = np.zeros((P, 640))
    z[:32] = bucket[None] == np.arange(32)[:, None]
    c["bucket"] = z
    at, n, parts = {}, 0, []
    for name, a in c.items():
        at[name] = (n, a.shape[1])
        n += a.shape[1]
        parts.append(a)
    return np.ascontiguousarray(np.concatenate(parts, 1).astype(np.float32)), at


class Machine(Program):

    def __init__(self, nc, adds_of, dram, const_at, plan):
        super().__init__(nc, adds_of)
        self.dram, self.plan = dram, plan
        self.col_at, self.ncols, _ = column_plan()
        self.const_at = const_at
        self.x = nc.alloc_sbuf_tensor("x", [P, KT, T], F32)
        self.cols = nc.alloc_sbuf_tensor("cols", [P, self.ncols], F32)
        self.const = nc.alloc_sbuf_tensor("const", [P, sum(n for _, n in const_at.values())], F32)
        self.slots = [nc.alloc_sbuf_tensor(f"slot{s}", [P, SLOT * P], F32) for s in (0, 1)]
        self.bank = [nc.alloc_psum_tensor(f"bank{b}", [P, T], F32) for b in range(8)]
        self.loaded = [Count(self, f"slot_loaded{s}") for s in (0, 1)]
        self.slot_free = [Count(self, f"slot_free{s}", nc.tensor) for s in (0, 1)]
        self.freed = [Count(self, f"set_freed{s}", nc.vector) for s in (0, 1)]
        self.taken, self.toggle = 0, 0
        self.slot_trips = []
        t = [self.dma(self.x[:], dram["x"].rearrange("(k p) t -> p k t", p=P)),
             self.dma(self.cols[:], dram["cols"]), self.dma(self.const[:], dram["const"])]
        for e in self.compute:
            e.after(*t)

    def c(self, name, a=0, b=None):
        n0, w = self.const_at[name]
        return self.const[:, n0 + a:n0 + (w if b is None else b)]

    def col(self, name, k=0):
        k = k + self.col_at[name]
        return self.cols[:, k:k + 1] if isinstance(k, int) else self.cols[:, bass.ds(k, 1)]

    @contextmanager
    def buffers(self, **shapes):
        with ExitStack() as st:
            self.ndma += 1
            yield {k: st.enter_context(self.nc.sbuf_tensor(f"{k}_{self.ndma}", [P, *v], F32)) for k, v in shapes.items()}
            self.join()

    def take(self):
        s, self.toggle = self.toggle, 1 - self.toggle
        here = self.taken
        index = here
        for lp, first in zip(self.loops, self.slot_trips):
            index = index + lp.reg * first
        nb = len(self.plan[here])
        self.taken += 1
        self.sp.wait(self.slot_free[s].now())
        src = self.dram["wstream"]
        src = src[index, :, 0:nb * P] if isinstance(index, int) else \
            src[bass.ds(index, 1), :, 0:nb * P].rearrange("o p n -> p (o n)")
        t = self.loaded[s].add(self.sp.eng.dma_start(self.slots[s][:, 0:nb * P], src), 16)
        self.pe.after(t)
        return s, self.slots[s].rearrange("p (b n) -> p b n", n=P)

    @contextmanager
    def weight_loop(self, trips, slots):
        assert slots % 2 == 0
        first = self.taken
        with self.loop(trips) as i:
            self.slot_trips.append(slots)
            yield i
            self.slot_trips.pop()
            assert self.taken - first == slots, (self.taken - first, slots)
        for t in range(trips):
            for k in range(slots):
                assert len(self.plan[first + t * slots + k]) == len(self.plan[first + k])
        self.taken = first + trips * slots

    def mm(self, out, w, rhs, start=True, stop=True):
        return self.pe.eng.matmul(out, w, rhs, start=start, stop=stop, skip_group_check=True)

    def project(self, out, blocks, rhs, free=None, start=True, stop=True):
        for k, (b, r) in enumerate(zip(blocks, rhs)):
            ins = self.mm(out, b, r, start and k == 0, stop and k == len(blocks) - 1)
        return self.pe.do(ins, self.slot_free[free] if free is not None else None)

    def open_set(self, s, *tokens):
        self.pe.after(self.freed[s].now(), *tokens)

    def tiles(self, buf, n=KT):
        return [buf[:, k, :] for k in range(n)]

    def moment(self, src, n, sq, out_bank, lhs, square=True):
        a, pe = self.act, self.pe
        for k in range(n):
            if square:
                a.after()
                t = a.do(a.eng.activation(sq[:, k, :], src[:, k, :], ACT.Square))
                pe.after(t)
            ins = self.mm(out_bank, lhs, (sq if square else src)[:, k, :], k == 0, k == n - 1)
        return pe.do(ins)

    def inv_root(self, out, ss, token, scale, eps, floor=None):
        v, a = self.dve, self.act
        v.after(token)
        if floor is None:
            t = v.do(v.eng.tensor_scalar(out, ss, scale, eps, ALU.mult, ALU.add))
        else:
            t = v.do(v.eng.tensor_scalar(out, ss, floor, None, ALU.max))
        a.after(t)
        t = a.do(a.eng.activation(out, out, ACT.Sqrt))
        v.after(t)
        return v.do(v.eng.reciprocal(out, out))

    def rms(self, src, dst, gain, sq, rstd):
        self.join()
        t = self.moment(src, KT, sq, self.bank[7][:], self.c("ones"))
        self.inv_root(rstd[:], self.bank[7][:], t, 1.0 / D, 1e-6)
        v = self.dve
        for k in range(KT):
            v.after()
            t = v.do(v.eng.scalar_tensor_tensor(dst[:, k, :], src[:, k, :], self.col(gain, k), rstd[:], ALU.mult, ALU.mult))
        self.pe.after(t)
        return t

    def add_rms(self, y, gain, weight, sq, rstd):
        self.rms(y, y, gain, sq, rstd)
        v = self.dve
        for k in range(KT):
            v.after()
            v.do(v.eng.scalar_tensor_tensor(self.x[:, k, :], y[:, k, :], weight, self.x[:, k, :], ALU.mult, ALU.add))

    def gated_pairs(self, h, evacuate):
        with self.weight_loop(FT // 2, 2) as i:
            sg, g = self.take()
            tg = []
            for j in (0, 1):
                self.open_set(j)
                tg.append(self.project(self.bank[2 * j][:], [g[:, 8 * j + k, :] for k in range(KT)], self.tiles(h), sg if j else None))
            su, u = self.take()
            for j in (0, 1):
                tu = self.project(self.bank[2 * j + 1][:], [u[:, 8 * j + k, :] for k in range(KT)], self.tiles(h), su if j else None)
                evacuate(j, i * 2 + j, tg[j], tu)

    def down(self, act, y):
        half = FT // 2
        with self.weight_loop(KT // 2, 4) as i:
            for j in (0, 1):
                self.open_set(j)
                for part in (0, 1):
                    s, w = self.take()
                    t = self.project(self.bank[2 * j][:], [w[:, k, :] for k in range(half)],
                                     [act[:, part * half + k, :] for k in range(half)], s, part == 0, part == 1)
                self.evacuate(y, i * 2 + j, j, t)

    def evacuate(self, dst, k, j, t):
        a = self.act
        a.after(t)
        out = dst[:, k, :] if isinstance(k, int) else dst[:, bass.ds(k, 1), :].rearrange("p o t -> p (o t)")
        return a.do(a.eng.copy(out, self.bank[2 * j][:]), self.freed[j])

    def pair_units(self, rhs, w, s, evac):
        n = len(rhs)
        for j in (0, 1):
            self.open_set(j)
            t = self.project(self.bank[2 * j][:], [w[:, n * j + k, :] for k in range(n)], rhs, s if j else None)
            evac(j, t)

    def pairs(self, rhs, n, evac):
        def body(i):
            for q in (0, 1):
                s, w = self.take()
                self.pair_units(rhs, w, s, lambda j, t: evac(j, i * 4 + 2 * q + j, t))

        if n == 4:
            body(0)
        else:
            with self.weight_loop(n // 4, 2) as i:
                body(i)


def tile_of(buf, k, cols=slice(None)):
    if isinstance(k, int):
        return buf[:, k, cols]
    return buf[:, bass.ds(k, 1), cols].rearrange("p o t -> p (o t)")


def swiglu_block(m, pre, post):
    with m.buffers(h=[KT, T], act=[FT, T], sg=[2, T], sq=[KT, T], rstd=[T]) as b:
        m.rms(m.x, b["h"], pre, b["sq"], b["rstd"])

        def gate(j, k, tg, tu):
            a, v = m.act, m.dve
            a.after(tg)
            t = a.do(a.eng.activation(b["sg"][:, j, :], m.bank[2 * j][:], ACT.Silu))
            v.after(t, tu)
            v.do(v.eng.tensor_tensor(tile_of(b["act"], k), b["sg"][:, j, :], m.bank[2 * j + 1][:], ALU.mult), m.freed[j])

        m.gated_pairs(b["h"], gate)
        m.join()
        m.down(b["act"], b["h"])
        m.add_rms(b["h"], post, 0.5, b["sq"], b["rstd"])


def to_keys(m, src, dst, bank, tok, width=P):
    m.pe.after(tok)
    for k in range(TT):
        ins = m.pe.eng.transpose(bank[:, k * P:(k + 1) * P], src[:, k * P:(k + 1) * P], m.c("ident"))
    t = m.pe.do(ins)
    m.dve.after(t)
    return m.dve.do(m.dve.eng.tensor_copy(dst, bank[:].rearrange("p (k c) -> p k c", c=P) if width == P else
                                          bank[:].rearrange("p (k a c) -> p k a c", c=HD, a=2)))


def qkv_units(m, h, qT, kT, vT, order=lambda ap: ap):
    a, v = m.act, m.dve
    s, w = m.take()
    m.open_set(0)
    t = m.project(m.bank[0][:], [w[:, k, :] for k in range(KT)], m.tiles(h))
    a.after(t)
    tq = a.do(a.eng.mul(qT[:].rearrange("p (r a m) -> p r a m", r=4, a=4) if order is permuted else qT[:],
                        order(m.bank[0][:]), HD ** -0.5), m.freed[0])
    m.open_set(1)
    t = m.project(m.bank[2][:], [w[:, KT + k, :] for k in range(KT)], m.tiles(h), s)
    v.after(t)
    tk = v.do(v.eng.tensor_copy(kT[:].rearrange("p (r a m) -> p r a m", r=4, a=4) if order is permuted else kT[:],
                                order(m.bank[2][:])), m.freed[1])
    s, w = m.take()
    m.open_set(0)
    t = m.project(m.bank[0][:], [w[:, k, :] for k in range(KT)], m.tiles(h), s)
    a.after(t)
    tv = a.do(a.eng.copy(vT[:].rearrange("p (r a m) -> p r a m", r=4, a=4) if order is permuted else vT[:],
                         order(m.bank[0][:])), m.freed[0])
    return tq, tk, tv


def diff_attention(m, h, mix):
    a, v, pe = m.act, m.dve, m.pe
    with m.buffers(q=[T], k=[T], vT=[T], V=[TT, P], e=[2, T], pd=[T], pt=[TT, P], o=[T], sq=[1, T], rstd=[T], st=[16], lam=[8]) as b:
        lam = b["lam"]
        v.after()
        v.do(v.eng.tensor_tensor(lam[:, 0:2], m.cols[:, m.col_at["diff_lam_q1"]:m.col_at["diff_lam_q1"] + 2],
                                 m.cols[:, m.col_at["diff_lam_k1"]:m.col_at["diff_lam_k1"] + 2], ALU.mult))
        pe.after(v.last)
        t = pe.do(m.mm(m.bank[4][:, 0:2], m.c("ones"), lam[:, 0:2]))
        a.after(t)
        t = a.do(a.eng.activation(lam[:, 2:4], m.bank[4][:, 0:2], ACT.Exp))
        v.after(t)
        v.do(v.eng.tensor_tensor(lam[:, 4:5], lam[:, 3:4], lam[:, 2:3], ALU.subtract))
        v.after()
        v.do(v.eng.tensor_scalar(lam[:, 5:6], lam[:, 4:5], -LAM0, None, ALU.add))
        with m.weight_loop(4, 2) as head:
            tq, tk, tv = qkv_units(m, h, b["q"], b["k"], b["vT"])
            tV = to_keys(m, b["vT"], b["V"][:], m.bank[4], tv)
            pe.after(tq, tk, tV)
            st = b["st"]
            for i in range(TT):
                W = (i + 1) * P
                sb = [m.bank[4], m.bank[5]]
                ts = []
                if i:
                    pe.after(last_use)
                for c in (0, 1):
                    ts.append(pe.do(m.mm(sb[c][:, 0:W], b["q"][c * HD:(c + 1) * HD, i * P:W], b["k"][c * HD:(c + 1) * HD, 0:W])))
                for c in (0, 1):
                    v.after(ts[c])
                    v.do(v.eng.tensor_tensor(sb[c][:, i * P:W], sb[c][:, i * P:W], m.c("causal"), ALU.add))
                    v.after()
                    v.do(v.eng.reduce_max(st[:, c:c + 1], sb[c][:, 0:W], AX))
                    v.after()
                    t = v.do(v.eng.tensor_scalar(st[:, 2 + c:3 + c], st[:, c:c + 1], -1.0, None, ALU.mult))
                    a.after(t)
                    te = a.do(a.eng.activation(b["e"][:, c, 0:W], sb[c][:, 0:W], ACT.Exp, bias=st[:, 2 + c:3 + c],
                                               accum_out=st[:, 4 + c:5 + c]))
                last_use = te
                v.after(te)
                v.do(v.eng.reciprocal(st[:, 6:8], st[:, 4:6]))
                v.after()
                v.do(v.eng.tensor_tensor(st[:, 8:9], st[:, 7:8], lam[:, 5:6], ALU.mult))
                v.after()
                v.do(v.eng.tensor_scalar(b["pd"][:, 0:W], b["e"][:, 0, 0:W], st[:, 6:7], None, ALU.mult))
                v.after()
                t = v.do(v.eng.scalar_tensor_tensor(b["pd"][:, 0:W], b["e"][:, 1, 0:W], st[:, 8:9], b["pd"][:, 0:W], ALU.mult, ALU.add))
                pe.after(t)
                for k in range(i + 1):
                    ins = pe.eng.transpose(m.bank[6][:, k * P:(k + 1) * P], b["pd"][:, k * P:(k + 1) * P], m.c("ident"))
                t = pe.do(ins)
                v.after(t)
                t = v.do(v.eng.tensor_copy(b["pt"][:, 0:i + 1, :], m.bank[6][:, 0:W].rearrange("p (k c) -> p k c", c=P)))
                pe.after(t, tV)
                for k in range(i + 1):
                    ins = m.mm(m.bank[7][:, i * P:W], b["V"][:, k, :], b["pt"][:, k, :], k == 0, k == i)
                to = pe.do(ins)
            a.after(to)
            t = a.do(a.eng.copy(b["o"][:], m.bank[7][:]))
            a.after()
            t = a.do(a.eng.activation(b["sq"][:, 0, :], b["o"][:], ACT.Square))
            pe.after(t)
            t = pe.do(m.mm(m.bank[6][:], m.c("ones"), b["sq"][:, 0, :]))
            m.inv_root(b["rstd"][:], m.bank[6][:], t, 1.0 / P, 1e-5)
            v.after()
            v.do(v.eng.scalar_tensor_tensor(b["o"][:], b["o"][:], m.col("diff_subln_w"), b["rstd"][:], ALU.mult, ALU.mult))
            v.after()
            v.do(v.eng.tensor_scalar(tile_of(mix, head + 4), b["o"][:], 1.0 - LAM0, None, ALU.mult))
            m.join()


def rwkv_inputs(m, h, b):
    a, v, pe = m.act, m.dve, m.pe
    v.after()
    v.do(v.eng.memset(b["raw"][:, :, 0:1], 0.0))
    v.after()
    v.do(v.eng.memset(b["lora"][:], 0.0))
    a.after(v.last)

    def shifted(j, k, t, dst, rows=P):
        raw, dif = b["raw"][0:rows, j, :], b["dif"][0:rows, j, :]
        a.after(t)
        t = a.do(a.eng.copy(raw[:, 1:T + 1], m.bank[2 * j][0:rows, :]))
        v.after(t)
        v.do(v.eng.tensor_tensor(dif, raw[:, 0:T], raw[:, 1:T + 1], ALU.subtract))
        v.after()
        return v.do(v.eng.scalar_tensor_tensor(dst[0:rows], dif, m.col("shift_mu", k)[0:rows], raw[:, 1:T + 1], ALU.mult, ALU.add), m.freed[j])

    m.pairs(m.tiles(h), 12, lambda j, k, t: shifted(j, k, t, tile_of(b["rkv"], k)))
    lora = b["lora"]
    s, w = m.take()
    m.pair_units(m.tiles(h), w, s, lambda j, t: shifted(j, 12 + j, t, lora[:, j, :]))
    s, w = m.take()
    m.open_set(0)
    t = m.project(m.bank[0][0:32, :], [w[:, k, 0:32] for k in range(KT)], m.tiles(h), s)
    shifted(0, 14, t, lora[:, 2, :], 32)
    a.after(v.last)
    a.do(a.eng.activation(lora[0:64, 0, :], lora[0:64, 0, :], ACT.Tanh))
    a.after()
    tl = a.do(a.eng.activation(lora[:, 1:3, :], lora[:, 1:3, :], ACT.Sigmoid))
    s, w = m.take()
    pe.after(tl)
    for c in range(4):
        j = c % 2
        m.open_set(j)
        td = pe.do(m.mm(m.bank[2 * j][:], w[0:64, c, :], lora[0:64, 0, :]))
        ti = pe.do(m.mm(m.bank[2 * j + 1][:], w[64:P, c, :], lora[64:P, 0, :]))
        a.after(td)
        t = a.do(a.eng.activation(b["lw"][:, c, :], m.bank[2 * j][:], ACT.Sigmoid, bias=m.col("rwkv_w0", c)))
        v.after(t)
        v.do(v.eng.tensor_scalar(b["lw"][:, c, :], b["lw"][:, c, :], LOG_DECAY, None, ALU.mult))
        a.after(ti)
        a.do(a.eng.activation(b["iclr"][:, c, :], m.bank[2 * j + 1][:], ACT.Sigmoid, bias=m.col("rwkv_a0", c)), m.freed[j])
    for c in range(4):
        j = c % 2
        m.open_set(j)
        m.mm(m.bank[2 * j][:], w[:, 4 + c, :], lora[:, 1, :], True, False)
        t = pe.do(m.mm(m.bank[2 * j][:], w[0:32, 8 + c, :], lora[0:32, 2, :], False, True), m.slot_free[s] if c == 3 else None)
        m.evacuate(b["gate"], c, j, t)
    m.join()
    r, k, kk = b["rkv"][:, 0:4, :], b["rkv"][:, 4:8, :], b["kk"]
    sq, rs = b["tmp"], b["rs"]
    for c in range(4):
        v.after()
        v.do(v.eng.tensor_scalar(kk[:, c, :], k[:, c, :], m.col("rwkv_k_k", c), None, ALU.mult))
    a.after(v.last)
    t = a.do(a.eng.activation(sq[:], kk[:], ACT.Square))
    pe.after(t)
    for c in range(4):
        t = pe.do(m.mm(m.bank[4 + c][:], m.c("headones"), sq[:, c, :]))
    for c in range(4):
        m.inv_root(rs[:, c, :], m.bank[4 + c][:], t, None, None, 1e-24)
    v.after()
    v.do(v.eng.tensor_tensor(kk[:], kk[:], rs[:], ALU.mult))
    for c in range(4):
        v.after()
        v.do(v.eng.tensor_scalar(sq[:, c, :], b["iclr"][:, c, :], -1.0, m.col("rwkv_k_a", c), ALU.add, ALU.mult))
        v.after()
        v.do(v.eng.scalar_tensor_tensor(k[:, c, :], sq[:, c, :], 1.0, k[:, c, :], ALU.add, ALU.mult))
    for c in range(4):
        v.after()
        v.do(v.eng.scalar_tensor_tensor(sq[:, c, :], r[:, c, :], m.col("rwkv_r_k", c), k[:, c, :], ALU.mult, ALU.mult))
    pe.after(v.last)
    for c in range(4):
        t = pe.do(m.mm(m.bank[4 + c][:], m.c("headones"), sq[:, c, :]))
    for c in range(4):
        v.after(t)
        v.do(v.eng.tensor_tensor(b["bonus"][:, c, :], m.bank[4 + c][:], b["rkv"][:, 8 + c, :], ALU.mult))
    cum = b["tmp"]
    for c in range(4):
        v.after()
        v.do(v.eng.tensor_tensor_scan(cum[:, c, :], m.c("reset"), b["lw"][:, c, :], 0.0, ALU.mult, ALU.add))
    ch = lambda ap: ap.rearrange("p c (n l) -> p c n l", l=LC)
    a.after(v.last)
    tp = a.do(a.eng.activation(rs[:], cum[:], ACT.Exp))
    a.after()
    v.after()
    v.do(v.eng.tensor_tensor(b["lw"][:], cum[:], b["lw"][:], ALU.subtract))
    a.after(v.last)
    tx = a.do(a.eng.activation(b["lw"][:], b["lw"][:], ACT.Exp))
    v.after(tp)
    v.do(v.eng.tensor_copy(b["plast"][:], ch(rs[:])[:, :, :, LC - 1]))
    AR, BK = b["AR"], b["BK"]
    for c in range(4):
        one = lambda ap: ap[:, c, :].rearrange("p (n l) -> p n l", l=LC)
        v.after()
        v.do(v.eng.tensor_tensor(AR[:, c, :, LC:P], one(r), one(rs), ALU.mult))
        v.after(tx)
        v.do(v.eng.scalar_tensor_tensor(AR[:, c, :, 0:LC], one(kk), -1.0, one(b["lw"]), ALU.mult, ALU.mult))
    a.after(v.last)
    ti = a.do(a.eng.activation(rs[:], cum[:], ACT.Exp, scale=-1.0))
    v.after(ti)
    for c in range(4):
        one = lambda ap: ap[:, c, :].rearrange("p (n l) -> p n l", l=LC)
        v.after()
        v.do(v.eng.tensor_tensor(BK[:, c, :, LC:P], one(k), one(rs), ALU.mult))
        v.after()
        v.do(v.eng.tensor_tensor(kk[:, c, :], kk[:, c, :], b["iclr"][:, c, :], ALU.mult))
        v.after()
        v.do(v.eng.tensor_tensor(BK[:, c, :, 0:LC], one(kk), one(rs), ALU.mult))
    m.join()


def rwkv_chunks(m, b, yT):
    a, v, pe = m.act, m.dve, m.pe
    H8 = lambda bank: bank[0:LC, :].rearrange("p (h n) -> p h n", n=LC)
    bc = lambda name, n=8: m.c(name)[0:LC, :].unsqueeze(1).broadcast_to([LC, n, LC])
    v.after()
    v.do(v.eng.memset(b["X"][:], 0.0))
    v.after()
    v.do(v.eng.memset(b["vs"][:], 0.0))
    v.after()
    v.do(v.eng.memset(b["y"][:], 0.0))
    pe.after(v.last)
    a.after(v.last)
    B = m.bank
    place = lambda hd: hd % 2 * 4 + hd // 2
    with m.loop(NCH) as ci:
        ar, bk, vs = b["ar"], b["bk"], b["vs"]
        pick = lambda buf: buf[:, :, bass.ds(ci, 1), :].rearrange("p c o n -> p c (o n)")
        v.after()
        t_ar = v.do(v.eng.tensor_copy(ar[:], pick(b["AR"])))
        a.after()
        t_bk = a.do(a.eng.copy(bk[:], pick(b["BK"])))
        a.after()
        t_vs = a.do(a.eng.copy(vs[:, :, LC:P], b["rkv"][:, 8:12, bass.ds(ci * LC, LC)]))
        pe.after(t_ar, t_bk)
        for o in range(8):
            q = slice(o // 4 * HD, o // 4 * HD + HD)
            ins = m.mm(B[o // 4][:, (o % 4) * P:(o % 4 + 1) * P], bk[q, o % 4, :], ar[q, o % 4, :])
            if o % 4 == 3:
                t = pe.do(ins)
                v.after(t)
                v.do(v.eng.tensor_tensor(b["G"][:, o - 3:o + 1, :], B[o // 4][:].rearrange("p (h n) -> p h n", n=P),
                                         m.c("pairmask").unsqueeze(1).broadcast_to([P, 4, P]), ALU.mult))
        for o in range(8):
            q = slice(o // 4 * HD, o // 4 * HD + HD)
            ins = m.mm(B[(2, 5)[o // 4]][0:LC, (o % 4) * LC:(o % 4 + 1) * LC], ar[q, o % 4, 0:LC], bk[q, o % 4, 0:LC])
        tn = pe.do(ins)
        for c in range(4):
            ins = pe.eng.transpose(B[3][:, c * P:(c + 1) * P], bk[:, c, :], m.c("ident"))
        t = pe.do(ins)
        a.after(t)
        t_bkt = a.do(a.eng.copy(b["bkt"][:], B[3][:]))
        pe.after(t_vs)
        for c in range(4):
            ins = pe.eng.transpose(B[4][:, c * P:(c + 1) * P], vs[:, c, :], m.c("ident"))
        t = pe.do(ins)
        a.after(t)
        t_v = a.do(a.eng.copy(b["UV"][LC:P, :], B[4][LC:P, :]))
        N, NT, W, WT = b["N"], b["NT"], b["W"], b["WT"]
        near, near_t, far = b["near"], b["near_t"], b["far"]
        v.after(tn)
        for e, bank in enumerate((B[2], B[5])):
            half = bank[0:LC, 0:4 * LC].rearrange("p (h n) -> p h n", n=LC)
            v.after()
            v.do(v.eng.tensor_tensor(near_t[0:LC, 4 * e:4 * e + 4, :], half, bc("near_t", 4), ALU.mult))
        n_of = b["G"][0:LC, :, 0:LC]
        v.after()
        v.do(v.eng.tensor_tensor(near[0:LC], n_of, bc("near"), ALU.mult))
        v.after()
        v.do(v.eng.tensor_tensor(far[0:LC], n_of, bc("far"), ALU.mult))
        v.after()
        v.do(v.eng.tensor_tensor(W[0:LC], near[0:LC], bc("ident64"), ALU.add))
        v.after()
        v.do(v.eng.tensor_tensor(WT[0:LC], near_t[0:LC], bc("ident64"), ALU.add))

        def product(bank, lhs, rhs, *tokens):
            pe.after(*tokens)
            m.mm(bank[:, 0:2], m.c("ident"), m.c("ident", 0, 2))
            for hd in range(8):
                ins = m.mm(bank[0:LC, hd * LC:(hd + 1) * LC], lhs[0:LC, hd, :], rhs[0:LC, hd, :])
            return pe.do(ins)

        cur, cur_t, ready = near, near_t, v.last
        for step in range(3):
            nxt, nxt_t = (N, NT) if step % 2 == 0 else (near, near_t)
            t1 = product(B[5], cur_t, cur, ready)
            t2 = product(B[6], cur, cur_t)
            a.after(t1)
            ta = a.do(a.eng.copy(nxt[0:LC], H8(B[5])))
            v.after(t2)
            tb = v.do(v.eng.tensor_copy(nxt_t[0:LC], H8(B[6])))
            t1 = product(B[7], nxt_t, W, ta, tb)
            t2 = product(B[2], nxt, WT)
            v.after(t1)
            v.do(v.eng.tensor_tensor(W[0:LC], H8(B[7]), W[0:LC], ALU.add))
            v.after(t2)
            ready = v.do(v.eng.tensor_tensor(WT[0:LC], H8(B[2]), WT[0:LC], ALU.add))
            cur, cur_t = nxt, nxt_t
        E, ET, E2T = b["near"], b["near_t"], b["N"]
        t1 = product(B[5], WT, far, ready)
        t2 = product(B[6], far, WT)
        a.after(t1)
        ta = a.do(a.eng.copy(E[0:LC], H8(B[5])))
        v.after(t2)
        tb = v.do(v.eng.tensor_copy(ET[0:LC], H8(B[6])))
        t1 = product(B[7], E, ET, ta, tb)
        a.after(t1)
        ta = a.do(a.eng.copy(E2T[0:LC], H8(B[7])))
        t1 = product(B[5], E2T, W, ta)
        v.after(t1)
        tb = v.do(v.eng.tensor_tensor(W[0:LC], H8(B[5]), W[0:LC], ALU.add))
        t1 = product(B[6], ET, W, tb)
        v.after(t1)
        t_w = v.do(v.eng.tensor_tensor(W[0:LC], H8(B[6]), W[0:LC], ALU.add))
        X, UV, G = b["X"], b["UV"], b["G"]
        pe.after(t_v, t_w)
        for c in range(4):
            m.mm(B[0][0:LC, c * P:(c + 1) * P], ar[:, c, 0:LC], X[:, c, :], True, False)
            for hd in (2 * c, 2 * c + 1):
                ins = m.mm(B[0][0:LC, hd * LC:(hd + 1) * LC], G[LC:P, place(hd), 0:LC], UV[LC:P, hd * LC:(hd + 1) * LC], False, hd % 2 == 1)
        t = pe.do(ins)
        v.after(t)
        t = v.do(v.eng.tensor_copy(b["Z"][0:LC].rearrange("p (e c) n -> p c e n", e=2), B[0][0:LC, :].rearrange("p (c e n) -> p c e n", e=2, n=LC)))
        t = product(B[1], W, b["Z"], t)
        v.after(t)
        t_u = v.do(v.eng.tensor_copy(UV[0:LC, :].rearrange("p (c e n) -> p c e n", e=2, n=LC), B[1][0:LC, :].rearrange("p (e c n) -> p c e n", e=2, n=LC)))
        pe.after(t_u, t_bkt)
        for c in range(4):
            m.mm(B[2][0:LC, c * P:(c + 1) * P], ar[:, c, LC:P], X[:, c, :], True, False)
            for hd in (2 * c, 2 * c + 1):
                ins = m.mm(B[2][0:LC, hd * LC:(hd + 1) * LC], G[:, place(hd), LC:P], UV[:, hd * LC:(hd + 1) * LC], False, hd % 2 == 1)
        t_y = pe.do(ins)
        for c in range(4):
            ins = m.mm(B[3][:, c * P:(c + 1) * P], b["bkt"][:, c * P:(c + 1) * P], UV[:, c * P:(c + 1) * P])
        t_x = pe.do(ins)
        a.after(t_y)
        t_ys = a.do(a.eng.copy(b["y"][0:LC, :], B[2][0:LC, :]))
        v.after(t_x)
        v.do(v.eng.tensor_tensor(X[:], B[3][:].rearrange("p (c n) -> p c n", n=P), X[:], ALU.add))
        v.after()
        v.do(v.eng.tensor_tensor(X[:], X[:], m.c("headones").unsqueeze(1).broadcast_to([P, 4, P]), ALU.mult))
        for c in range(4):
            v.after()
            v.do(v.eng.tensor_scalar(X[:, c, :], X[:, c, :],
                                     b["plast"][:, c, bass.ds(ci, 1)], None, ALU.mult))
        pe.after(t_ys)
        for c in range(4):
            ins = pe.eng.transpose(B[4][:, c * P:(c + 1) * P], b["y"][:, c * P:(c + 1) * P], m.c("ident"))
        t = pe.do(ins)
        a.after(t)
        a.do(a.eng.copy(yT[:, :, bass.ds(ci * LC, LC)], B[4][:].rearrange("p (c l) -> p c l", l=P)[:, :, 0:LC]))
        m.join()


def rwkv(m, h, mix):
    a, v, pe = m.act, m.dve, m.pe
    with m.buffers(rkv=[12, T], gate=[4, T], bonus=[4, T], AR=[4, NCH, P], BK=[4, NCH, P], plast=[4, NCH]) as b:
        with m.buffers(raw=[2, T + 1], dif=[2, T], lora=[3, T], lw=[4, T], iclr=[4, T], kk=[4, T], tmp=[4, T], rs=[4, T]) as b2:
            rwkv_inputs(m, h, {**b, **b2})
        with m.buffers(yT=[4, T], X=[4, P], ar=[4, P], bk=[4, P], vs=[4, P], G=[8, P], bkt=[T], UV=[T], N=[8, LC], NT=[8, LC],
                       W=[8, LC], WT=[8, LC], near=[8, LC], near_t=[8, LC], far=[8, LC], Z=[8, LC], y=[T]) as b3:
            yT = b3["yT"]
            rwkv_chunks(m, {**b, **b3}, yT)
            flat = lambda buf: buf.rearrange("p c n l -> p (c n l)")
            dev, sq = (flat(b["AR"])[:, n * 4 * T:(n + 1) * 4 * T].rearrange("p (c t) -> p c t", t=T) for n in (0, 1))
            rs = flat(b["BK"])[:, 0:4 * T].rearrange("p (c t) -> p c t", t=T)
            for c in range(4):
                t = pe.do(m.mm(m.bank[4 + c][:], m.c("headones"), yT[:, c, :]))
            for c in range(4):
                v.after(t)
                v.do(v.eng.scalar_tensor_tensor(dev[:, c, :], m.bank[4 + c][:], -1.0 / HD, yT[:, c, :], ALU.mult, ALU.add))
            a.after(v.last)
            t = a.do(a.eng.activation(sq[:], dev[:], ACT.Square))
            pe.after(t)
            for c in range(4):
                t = pe.do(m.mm(m.bank[4 + c][:], m.c("headones"), sq[:, c, :]))
            for c in range(4):
                m.inv_root(rs[:, c, :], m.bank[4 + c][:], t, 1.0 / HD, 64e-5)
            for c in range(4):
                v.after()
                v.do(v.eng.scalar_tensor_tensor(dev[:, c, :], dev[:, c, :], m.col("rwkv_gn_w", c), rs[:, c, :], ALU.mult, ALU.mult))
                v.after()
                v.do(v.eng.scalar_tensor_tensor(dev[:, c, :], dev[:, c, :], m.col("rwkv_gn_b", c), b["bonus"][:, c, :], ALU.add, ALU.add))
            v.after()
            v.do(v.eng.tensor_tensor(mix[:, 0:4, :], dev[:], b["gate"][:], ALU.mult))
            m.join()


def block1(m):
    swiglu_block(m, "ffn1_pre_g", "ffn1_post_g")
    with m.buffers(mix=[KT, T]) as bm:
        with m.buffers(h=[KT, T]) as bh:
            with m.buffers(sq=[KT, T], rstd=[T]) as b:
                m.rms(m.x, bh["h"], "mix_pre_g", b["sq"], b["rstd"])
                m.join()
            diff_attention(m, bh["h"], bm["mix"])
            rwkv(m, bh["h"], bm["mix"])
        with m.buffers(y=[KT, T], sq=[KT, T], rstd=[T]) as b:
            m.pe.after(m.dve.last)
            m.pairs(m.tiles(bm["mix"]), KT, lambda j, k, t: m.evacuate(b["y"], k, j, t))
            m.add_rms(b["y"], "mix_post_g", 1.0, b["sq"], b["rstd"])
    swiglu_block(m, "ffn2_pre_g", "ffn2_post_g")


def pool_mixer(m, y):
    a, v, pe = m.act, m.dve, m.pe
    PAD = 16
    with m.buffers(act=[16, T], u=[2, PAD + T], wa=[PAD + T], wb=[PAD + T], pooled=[4, T], mixed=[4, T], sg=[2, T]) as b:
        v.after()
        v.do(v.eng.memset(b["u"][:], 0.0))
        a.after(v.last)
        xs = m.tiles(m.x)
        for g, w in enumerate((2, 4, 8, 16)):
            def window(j, k, t):
                u = b["u"][:, j, :]
                a.after(t)
                t = a.do(a.eng.copy(u[:, PAD:], m.bank[2 * j][:]))
                cur, step, n = u, 1, 0
                v.after(t)
                while step < w:
                    nxt = (b["wa"], b["wb"])[n % 2][:]
                    lo = 2 * step - 1
                    v.after()
                    v.do(v.eng.tensor_tensor(nxt[:, lo:], cur[:, lo:], cur[:, lo - step:PAD + T - step], ALU.add))
                    cur, step, n = nxt, 2 * step, n + 1
                v.after()
                v.do(v.eng.scalar_tensor_tensor(b["pooled"][:, k, PAD:], cur[:, 2 * PAD:], 1.0 / w, u[:, 2 * PAD:], ALU.mult, ALU.subtract))
                v.after()
                v.do(v.eng.tensor_tensor(cur[:, PAD:2 * PAD], cur[:, PAD:2 * PAD], m.c("early", 16 * g, 16 * g + 16), ALU.mult))
                v.after()
                v.do(v.eng.tensor_tensor(b["pooled"][:, k, 0:PAD], cur[:, PAD:2 * PAD], u[:, PAD:2 * PAD], ALU.subtract), m.freed[j])

            m.pairs(xs, 4, window)
            pe.after(v.last)
            s, wg = m.take()
            for k in range(4):
                j = k % 2
                m.open_set(j)
                t = m.project(m.bank[2 * j][:], [wg[:, 4 * k + c, :] for c in range(4)], m.tiles(b["pooled"], 4), s if k == 3 else None)
                a.after(t)
                a.do(a.eng.activation(b["mixed"][:, k, :], m.bank[2 * j][:], ACT.Copy, scale=m.col("scale_a_2", 4 * g + k)), m.freed[j])
            t_mixed = a.last

            def gate(j, k, t):
                a.after(t)
                t = a.do(a.eng.activation(b["sg"][:, j, :], m.bank[2 * j][:], ACT.Silu))
                v.after(t, t_mixed)
                v.do(v.eng.tensor_tensor(b["act"][:, 4 * g + k, :], b["sg"][:, j, :], b["mixed"][:, k, :], ALU.mult), m.freed[j])

            m.pairs(xs, 4, gate)
            a.after(v.last)
        pe.after(v.last)
        with m.weight_loop(KT // 2, 2) as i:
            for j in (0, 1):
                m.open_set(j)
                s, w = m.take()
                t = m.project(m.bank[2 * j][:], [w[:, k, :] for k in range(16)], m.tiles(b["act"], 16), s)
                m.evacuate(y, i * 2 + j, j, t)


def layer_norm(m, y, l, sq, rstd):
    v, a, pe = m.dve, m.act, m.pe
    m.join()
    for k in range(KT):
        v.after()
        v.do(v.eng.scalar_tensor_tensor(y[:, k, :], m.x[:, k, :], ALPHA, y[:, k, :], ALU.mult, ALU.add))
    pe.after(v.last)
    t = m.moment(y, KT, None, m.bank[6][:], m.c("ones"), square=False)
    v.after(t)
    v.do(v.eng.tensor_scalar(rstd[:], m.bank[6][:], 1.0 / D, None, ALU.mult))
    for k in range(KT):
        v.after()
        v.do(v.eng.tensor_tensor(y[:, k, :], y[:, k, :], rstd[:], ALU.subtract))
    a.after(v.last)
    t = m.moment(y, KT, sq, m.bank[7][:], m.c("ones"))
    m.inv_root(rstd[:], m.bank[7][:], t, 1.0 / D, 1e-5)
    for k in range(KT):
        v.after()
        v.do(v.eng.scalar_tensor_tensor(y[:, k, :], y[:, k, :], m.col("ln_g_2", 8 * l + k), rstd[:], ALU.mult, ALU.mult))
        v.after()
        v.do(v.eng.tensor_scalar(m.x[:, k, :], y[:, k, :], m.col("ln_b_2", 8 * l + k), None, ALU.add))
    m.join()


def values_with_ones(m, b, tv):
    return to_keys(m, b["vT"], b["V"].rearrange("p k (a c) -> p k a c", a=2)[:, :, :, 0:HD], m.bank[6], tv, HD)


def dilated_group(m, g, b, O):
    a, v, pe = m.act, m.dve, m.pe
    nt, kw = (2, 2 * P) if g == 0 else (4, P)
    V = b["V"].rearrange("p k (a c) -> p k a c", a=2)
    with m.weight_loop(8, 2) as pair:
        tq, tk, tv = qkv_units(m, m.x, b["q"], b["k"], b["vT"], (lambda ap: ap) if g == 0 else permuted)
        tV = values_with_ones(m, b, tv)
        pe.after(tq, tk, tV)
        busy = [None, None]
        for first in range(0, TT, nt):
            tok_s, tok_e, tok_p = [None, None], [None, None], [None, None]
            for e in (0, 1):
                hp = slice(e * HD, e * HD + HD)
                pe.after(busy[e])
                for n in range(nt):
                    i = first + n
                    if g == 0 and i == 0:
                        m.mm(m.bank[4 + e][:, 0:P], b["q"][hp, 0:P], b["k"][hp, 0:P])
                        ins = m.mm(m.bank[4 + e][:, P:2 * P], b["q"][hp, 0:P], b["k"][hp, 0:P])
                    else:
                        keys = slice((i - 1) * P, (i + 1) * P) if g == 0 else slice(i * P, (i + 1) * P)
                        ins = m.mm(m.bank[4 + e][:, n * kw:(n + 1) * kw], b["q"][hp, i * P:(i + 1) * P], b["k"][hp, keys])
                tok_s[e] = pe.do(ins)
            for e in (0, 1):
                S, st = b["S"][:, e, :].rearrange("p (n k) -> p n k", k=kw), b["st"][:, e, :]
                n0, _ = m.const_at["slopes"]
                slope = m.const[:, bass.ds(pair * 2 + (n0 + 16 * g + e), 1)]
                if g == 0 and first == 0:
                    n1, _ = m.const_at["dist0a"]
                    dist = m.const[:, n1:n1 + 4 * P].rearrange("p (n k) -> p n k", k=kw)
                else:
                    dist = m.c(f"dist{g}").unsqueeze(1).broadcast_to([P, nt, kw])
                score = m.bank[4 + e].rearrange("p (n k) -> p n k", k=kw)
                v.after(tok_s[e])
                v.do(v.eng.scalar_tensor_tensor(S, dist, slope, score, ALU.mult, ALU.add))
                v.after()
                v.do(v.eng.reduce_max(st[:, 0:nt], S, AX))
                v.after()
                v.do(v.eng.tensor_tensor(S, S, st[:, 0:nt].unsqueeze(2).broadcast_to([P, nt, kw]), ALU.subtract))
                a.after(v.last)
                tok_e[e] = a.do(a.eng.activation(b["E"][:, e, :], b["S"][:, e, :], ACT.Exp))
                v.after()
                v.do(v.eng.tensor_copy(O[:, first:first + nt, bass.ds(pair * 2 + e, 1), HD + 1:HD + 2].rearrange("p n o c -> p n (o c)"),
                                       st[:, 0:nt].unsqueeze(2)))
            for e in (0, 1):
                pe.after(tok_e[e])
                for k in range(4):
                    ins = pe.eng.transpose(m.bank[6 + e][:, k * P:(k + 1) * P], b["E"][:, e, k * P:(k + 1) * P], m.c("ident"))
                t = pe.do(ins)
                a.after(t)
                tok_p[e] = a.do(a.eng.copy(b["PT"][:, e, :], m.bank[6 + e][:]))
            for e in (0, 1):
                pe.after(tok_p[e])
                for n in range(nt):
                    i = first + n
                    out = m.bank[4 + e][:, n * (HD + 1):(n + 1) * (HD + 1)]
                    blocks = [(n, i)] if g else [(2 * n, i - 1), (2 * n + 1, i)][i == 0:]
                    for z, (blk, key) in enumerate(blocks):
                        ins = m.mm(out, b["PT"][:, e, blk * P:(blk + 1) * P], V[:, key, e, :], z == 0, z == len(blocks) - 1)
                t = pe.do(ins)
                v.after(t)
                busy[e] = v.do(v.eng.tensor_copy(O[:, first:first + nt, bass.ds(pair * 2 + e, 1), 0:HD + 1].rearrange("p n o c -> p n (o c)"),
                                                 m.bank[4 + e][:, 0:nt * (HD + 1)].rearrange("p (n c) -> p n c", c=HD + 1)))
        m.join()


def dilated_mixer(m, y):
    a, v, pe = m.act, m.dve, m.pe
    W = HD + 2
    natural = m.nc.dram_tensor("group0_natural", (T, 16 * W), F32, kind="Internal").ap()
    with m.buffers(O0=[TT, 16, W], O1=[TT, 16, W], O2=[TT, 16, W], gate=[KT, T]) as bo:
        with m.buffers(q=[T], k=[T], vT=[T], V=[TT, 2 * (HD + 1)], S=[2, T], E=[2, T], PT=[2, T], st=[2, 4]) as b:
            v.after()
            v.do(v.eng.memset(b["V"][:], 1.0))
            dilated_group(m, 0, b, bo["O0"])
            rows = lambda buf: buf.rearrange("p n h c -> p n (h c)")
            out = m.dma(natural.rearrange("(n p) c -> p n c", p=P), rows(bo["O0"]), [v.last], m.pool)
            back = natural.rearrange("(m a r) c -> a m r c", a=4, r=4)
            back_at = [m.dma(rows(bo["O0"])[32 * k:32 * k + 32], back[k], [out], m.pool) for k in range(4)]
            dilated_group(m, 1, b, bo["O1"])
            dilated_group(m, 2, b, bo["O2"])

        def gate(j, k, t):
            a.after(t)
            a.do(a.eng.activation(tile_of(bo["gate"], k), m.bank[2 * j][:], ACT.Silu), m.freed[j])

        m.pairs(m.tiles(m.x), KT, gate)
        with m.buffers(top=[64], w=[3, 64], rec=[64], merged=[64, HD], mg=[KT, T]) as b:
            O = [bo[f"O{g}"].rearrange("p n h c -> p (n h) c") for g in range(3)]
            v.after(*back_at)
            v.do(v.eng.tensor_tensor(b["top"][:], O[0][:, :, HD + 1], O[1][:, :, HD + 1], ALU.max))
            v.after()
            v.do(v.eng.tensor_tensor(b["top"][:], b["top"][:], O[2][:, :, HD + 1], ALU.max))
            for g in range(3):
                v.after()
                v.do(v.eng.tensor_tensor(b["w"][:, g, :], O[g][:, :, HD + 1], b["top"][:], ALU.subtract))
            a.after(v.last)
            t = a.do(a.eng.activation(b["w"][:], b["w"][:], ACT.Exp))
            v.after(t)
            for g in range(3):
                v.after()
                v.do(v.eng.tensor_tensor(O[g][:, :, 0:HD + 1], O[g][:, :, 0:HD + 1], b["w"][:, g, :].unsqueeze(2).broadcast_to([P, 64, HD + 1]), ALU.mult))
            for g in (1, 2):
                v.after()
                v.do(v.eng.tensor_tensor(O[0][:, :, 0:HD + 1], O[0][:, :, 0:HD + 1], O[g][:, :, 0:HD + 1], ALU.add))
            v.after()
            v.do(v.eng.reciprocal(b["rec"][:], O[0][:, :, HD]))
            v.after()
            t = v.do(v.eng.tensor_tensor(b["merged"][:], O[0][:, :, 0:HD], b["rec"][:].unsqueeze(2).broadcast_to([P, 64, HD]), ALU.mult))
            rows = b["merged"].rearrange("p (n h) c -> p n (h c)", n=TT)
            m.join()
            read = []
            for c in range(KT):
                bank = m.bank[4 + c % 4]
                pe.after(read[c - 4] if c >= 4 else None)
                for n in range(TT):
                    ins = pe.eng.transpose(bank[:, n * P:(n + 1) * P], rows[:, n, c * P:(c + 1) * P], m.c("ident"))
                t = pe.do(ins)
                v.after(t)
                read.append(v.do(v.eng.tensor_tensor(permuted(b["mg"][:, c, :]), bank[:].rearrange("p (r a m) -> p r a m", r=4, a=4),
                                                     permuted(bo["gate"][:, c, :]), ALU.mult)))
            pe.after(v.last)
            m.pairs(m.tiles(b["mg"]), KT, lambda j, k, t: m.evacuate(y, k, j, t))


def block2(m):
    with m.buffers(y=[KT, T], rstd=[T]) as b:
        for l, mixer in enumerate((pool_mixer, dilated_mixer)):
            mixer(m, b["y"])
            with m.buffers(sq=[KT, T]) as b2:
                layer_norm(m, b["y"], l, b2["sq"], b["rstd"])


def mlstm(m, h, mix):
    a, v, pe = m.act, m.dve, m.pe
    with m.buffers(qk=[4, T], og=[4, T], MV=[TT, 4 * P], ct=[TT, 4]) as b:
        with m.buffers(raw=[2, T + 3], vT=[2, T], lf=[T], z=[T], tmp=[T], one=[T], B=[T], cs=[T], nmu=[T], arg=[T]) as c:
            v.after()
            v.do(v.eng.memset(c["raw"][:], 0.0))
            a.after(v.last)

            def conv(j, k, t):
                raw = c["raw"][:, j, :]
                acc = b["qk"][:, k, :]
                a.after(t)
                t = a.do(a.eng.copy(raw[:, 3:], m.bank[2 * j][:]))
                v.after(t)
                v.do(v.eng.tensor_scalar(acc, raw[:, 0:T], m.col("mlstm_conv_w_3", k), m.col("mlstm_conv_b_3", k), ALU.mult, ALU.add))
                for tap in (1, 2, 3):
                    v.after()
                    v.do(v.eng.scalar_tensor_tensor(acc, raw[:, tap:tap + T], m.col("mlstm_conv_w_3", 4 * tap + k), acc, ALU.mult, ALU.add))
                a.after(v.last)
                t = a.do(a.eng.activation(acc, acc, ACT.Silu))
                v.after(t)
                v.do(v.eng.tensor_scalar(acc, acc, HD ** -0.5 if k < 2 else 1.0, None, ALU.mult), m.freed[j])

            m.pairs(m.tiles(h), 4, conv)

            def value(j, k, t):
                a.after(t)
                t = a.do(a.eng.copy(c["vT"][:, j, :], m.bank[2 * j][:]), m.freed[j])
                pe.after(v.last)
                to_keys(m, c["vT"][:, j, :], b["MV"][:, :, k * P:(k + 1) * P], m.bank[4], t)

            m.pairs(m.tiles(h), 4, value)
            m.pairs(m.tiles(h), 4, lambda j, k, t: (a.after(t), a.do(a.eng.activation(b["og"][:, k, :], m.bank[2 * j][:], ACT.Sigmoid), m.freed[j])))
            s, w = m.take()
            m.open_set(0)
            ti = m.project(m.bank[0][0:4, :], [w[:, k, 0:4] for k in range(KT)], m.tiles(h))
            tf = m.project(m.bank[1][0:4, :], [w[:, k, 4:8] for k in range(KT)], m.tiles(h))
            m.open_set(1)
            for n in range(TT):
                tw = m.project(m.bank[2][:, 8 * n:8 * n + 8], [h[:, k, n * P:(n + 1) * P] for k in range(KT)],
                               [w[:, KT + k, 0:8] for k in range(KT)], s if n == TT - 1 else None)
            v.after(tw)
            v.do(v.eng.tensor_scalar(m.iw[:], m.bank[2][:, 0:8 * TT], 8 ** -0.5, None, ALU.mult), m.freed[1])
            r = slice(0, 4)
            for name in ("cs", "nmu", "arg"):
                v.after()
                v.do(v.eng.memset(c[name][:], 0.0))
            v.after()
            v.do(v.eng.memset(c["one"][:], 1.0))
            z, tmp, lf = c["z"][r], c["tmp"][r], c["lf"][r]
            v.after(tf)
            v.do(v.eng.tensor_scalar(z, m.bank[1][r, :], m.col("f_bias_3")[r], None, ALU.add))
            v.after()
            v.do(v.eng.scalar_tensor_tensor(tmp, z, -1.0, z, ALU.mult, ALU.min))
            a.after(v.last)
            t = a.do(a.eng.activation(tmp, tmp, ACT.Exp))
            v.after(t)
            v.do(v.eng.tensor_scalar(tmp, tmp, 1.0, None, ALU.add))
            a.after(v.last)
            t = a.do(a.eng.activation(tmp, tmp, ACT.Ln))
            v.after(t)
            v.do(v.eng.scalar_tensor_tensor(lf, z, 0.0, tmp, ALU.min, ALU.subtract))
            v.after()
            v.do(v.eng.tensor_tensor_scan(c["B"][r], c["one"][r], lf, 0.0, ALU.mult, ALU.add))
            v.after(ti)
            v.do(v.eng.scalar_tensor_tensor(c["cs"][r], m.bank[0][r, :], m.col("i_bias_3")[r], c["B"][r], ALU.add, ALU.subtract), m.freed[0])
            v.after()
            v.do(v.eng.tensor_tensor_scan(tmp, c["one"][r], c["cs"][r], 0.0, ALU.mult, ALU.max))
            v.after()
            v.do(v.eng.tensor_scalar(c["nmu"][r], tmp, -1.0, None, ALU.mult))
            v.after()
            v.do(v.eng.tensor_tensor(c["arg"][r], c["nmu"][r], c["B"][r], ALU.subtract))
            pe.after(v.last)
            for n in range(TT):
                ins = pe.eng.transpose(m.bank[4][:, n * P:(n + 1) * P], c["cs"][:, n * P:(n + 1) * P], m.c("ident"))
            t = pe.do(ins)
            v.after(t)
            v.do(v.eng.tensor_copy(b["ct"][:], m.bank[4][:].rearrange("p (n c) -> p n c", c=P)[:, :, 0:4]))
            m.join()
            mlstm_heads(m, b, c["nmu"], c["arg"], mix)


def mlstm_heads(m, b, nmu, arg, mix):
    a, v, pe = m.act, m.dve, m.pe
    with m.buffers(mub=[T], md=[TT, P], thr=[T], E=[2, T], sc=[2, T], den=[T], hm=[T], sq=[T], rstd=[T]) as c:
        for hd in range(4):
            hp = slice(hd % 2 * HD, hd % 2 * HD + HD)
            pick = m.c("pick", hd * P, (hd + 1) * P)
            t1 = pe.do(m.mm(m.bank[4][:], pick, nmu[:]))
            t2 = pe.do(m.mm(m.bank[5][:], pick, arg[:]))
            a.after(t1)
            t = a.do(a.eng.copy(c["mub"][:], m.bank[4][:]))
            a.after(t2)
            t_thr = a.do(a.eng.activation(c["thr"][:], m.bank[5][:], ACT.Exp))
            v.after(t)
            t_md = v.do(v.eng.tensor_tensor(c["md"][:], c["mub"].rearrange("p (n c) -> p n c", c=P),
                                            m.c("causal_t").unsqueeze(1).broadcast_to([P, TT, P]), ALU.add))
            a.after(t_md)
            used = [None, None]
            pe.after(t_thr)
            for j in range(TT):
                W, e = T - j * P, j % 2
                E, sc = c["E"][:, e, :], c["sc"][:, e, :]
                sb = m.bank[6 + e]
                pe.after(used[e])
                t = pe.do(m.mm(sb[:, 0:W], b["qk"][hp, 2 + hd // 2, j * P:(j + 1) * P], b["qk"][hp, hd // 2, j * P:T]))
                a.after(used[e])
                te = a.do(a.eng.activation(E[:, 0:P], c["md"][:, j, :], ACT.Exp, bias=b["ct"][:, j, hd:hd + 1]))
                if W > P:
                    a.after()
                    te = a.do(a.eng.activation(E[:, P:W], c["mub"][:, (j + 1) * P:T], ACT.Exp, bias=b["ct"][:, j, hd:hd + 1]))
                v.after(t, te, pv if j >= 2 else None)
                used[e] = v.do(v.eng.tensor_tensor(sc[:, 0:W], E[:, 0:W], sb[:, 0:W], ALU.mult))
                pe.after(used[e])
                m.mm(m.bank[4][:, j * P:T], b["MV"][:, j, hd * P:(hd + 1) * P], sc[:, 0:W], j == 0, j == TT - 1)
                pv = pe.do(m.mm(m.bank[5][:, j * P:T], m.c("ones"), sc[:, 0:W], j == 0, j == TT - 1))
            v.after(pv, t_thr)
            v.do(v.eng.scalar_tensor_tensor(c["den"][:], m.bank[5][:], -1.0, c["thr"][:], ALU.mult, ALU.max))
            v.after()
            v.do(v.eng.tensor_tensor(c["den"][:], m.bank[5][:], c["den"][:], ALU.max))
            v.after()
            v.do(v.eng.reciprocal(c["den"][:], c["den"][:]))
            v.after()
            v.do(v.eng.tensor_tensor(c["hm"][:], m.bank[4][:], c["den"][:], ALU.mult))
            a.after(v.last)
            t = a.do(a.eng.activation(c["sq"][:], c["hm"][:], ACT.Square))
            pe.after(t)
            t = pe.do(m.mm(m.bank[5][:], m.c("ones"), c["sq"][:]))
            m.inv_root(c["rstd"][:], m.bank[5][:], t, 1.0 / P, 1e-6)
            v.after()
            v.do(v.eng.scalar_tensor_tensor(c["hm"][:], c["hm"][:], m.col("mlstm_norm_3", hd), c["rstd"][:], ALU.mult, ALU.mult))
            v.after()
            v.do(v.eng.tensor_tensor(mix[:, hd, :], c["hm"][:], b["og"][:, hd, :], ALU.mult))
            m.join()


def select_keys(m, h, sel):
    a, v, pe = m.act, m.dve, m.pe
    with m.buffers(kx=[T], qi=[4, T], sq=[T], rs=[T], rl=[2, T], top=[TT, 8]) as b:
        s, w = m.take()
        m.open_set(0)
        t = m.project(m.bank[0][:], [w[:, k, :] for k in range(KT)], m.tiles(h), s)
        m.evacuate(b["kx"].rearrange("p (o t) -> p o t", o=1), 0, 0, t)
        a.after()
        t = a.do(a.eng.activation(b["sq"][:], b["kx"][:], ACT.Square))
        pe.after(t)
        t = pe.do(m.mm(m.bank[4][:], m.c("headones"), b["sq"][:]))
        m.inv_root(b["rs"][:], m.bank[4][:], t, 1.0 / HD, 1e-6)
        v.after()
        t_k = v.do(v.eng.scalar_tensor_tensor(b["kx"][:], b["kx"][:], m.col("idx_k_norm_3"), b["rs"][:], ALU.mult, ALU.mult))
        m.pairs(m.tiles(h), 4, lambda j, k, t: (a.after(t), a.do(a.eng.mul(b["qi"][:, k, :], m.bank[2 * j][:], HD ** -0.5), m.freed[j])))
        pe.after(a.last, t_k)
        used, read = [None, None], [None, None]
        for n in range(1, TT):
            W = (n + 1) * P
            work = sel[:, n, 0:W]
            for hd in range(8):
                e = hd % 2
                hp = slice(e * HD, e * HD + HD)
                pe.after(used[e])
                t = pe.do(m.mm(m.bank[4 + e][:, 0:W], b["qi"][hp, hd // 2, n * P:W], b["kx"][hp, 0:W]))
                a.after(t, read[e])
                used[e] = a.do(a.eng.activation(b["rl"][:, e, 0:W], m.bank[4 + e][:, 0:W], ACT.Relu))
                v.after(used[e])
                wgt = m.iw[:, 8 * n + hd:8 * n + hd + 1]
                if hd == 0:
                    read[e] = v.do(v.eng.tensor_scalar(work, b["rl"][:, e, 0:W], wgt, 0.0, ALU.mult, ALU.add))
                else:
                    read[e] = v.do(v.eng.scalar_tensor_tensor(work, b["rl"][:, e, 0:W], wgt, work, ALU.mult, ALU.add))
            v.after()
            v.do(v.eng.tensor_tensor(sel[:, n, n * P:W], sel[:, n, n * P:W], m.c("causal"), ALU.add))
        for _ in range(TOPK // 8):
            for n in range(1, TT):
                work = sel[:, n, 0:(n + 1) * P]
                v.after()
                v.do(v.eng.max(b["top"][:, n, :], work))
                v.after()
                v.do(v.eng.match_replace(work, b["top"][:, n, :], work, TAKEN))
        for n in range(1, TT):
            work = sel[:, n, 0:(n + 1) * P]
            v.after()
            v.do(v.eng.tensor_scalar(work, work, 0.5 * TAKEN, NEG, ALU.is_gt, ALU.mult))
        v.after()
        v.do(v.eng.tensor_copy(sel[:, 0, 0:P], m.c("causal")))


def dsa(m, h, mix):
    a, v, pe = m.act, m.dve, m.pe
    line = m.nc.dram_tensor("bias_by_distance", (8, 640), F32, kind="Internal").ap()
    with m.buffers(sel=[TT, T], bias=[8, T]) as bs:
        with m.buffers(rb=[8], line=[640], skew=[8, T]) as b:
            everyone = [e.last for e in m.compute if e.last]
            t = m.dma(b["rb"][:], m.dram["rel_bias"], everyone, m.pool)
            pe.after(t)
            m.mm(m.bank[4][0:8, :], b["rb"][:], m.c("bucket", 0, T))
            t = pe.do(m.mm(m.bank[5][0:8, 0:P], b["rb"][:], m.c("bucket", T, T + P)))
            v.after(t)
            v.do(v.eng.tensor_copy(b["line"][0:8, 0:T], m.bank[4][0:8, :]))
            v.after()
            v.do(v.eng.tensor_copy(b["line"][0:8, T:T + P], m.bank[5][0:8, 0:P]))
            t = m.dma(line, b["line"][0:8, :], [v.last], m.pool)
            skewed = bass.AP(line.tensor, 0, [[1, P], [640, 8], [1, T]])
            t = m.dma(b["skew"][:], skewed, [t], m.pool)
            pe.after(t)
            got = []
            for hd in range(8):
                bank = m.bank[4 + hd % 4]
                pe.after(got[hd - 4] if hd >= 4 else None)
                t = pe.do(m.mm(bank[:], m.c("anti"), b["skew"][:, hd, :]))
                a.after(t)
                got.append(a.do(a.eng.copy(bs["bias"][:, hd, :], bank[:])))
        select_keys(m, h, bs["sel"])
        sel = bs["sel"]
        with m.buffers(q=[T], k=[T], vT=[T], V=[TT, 2 * (HD + 1)], S=[2, T], E=[2, T], PT=[2, T], st=[2, 4], o=[2, P]) as b:
            V = b["V"].rearrange("p k (a c) -> p k a c", a=2)
            v.after()
            v.do(v.eng.memset(b["V"][:], 1.0))
            with m.weight_loop(4, 2) as pair:
                tq, tk, tv = qkv_units(m, h, b["q"], b["k"], b["vT"])
                tV = values_with_ones(m, b, tv)
                pe.after(tq, tk, tV)
                busy = [None, None]
                for i in range(TT):
                    W = (i + 1) * P
                    tok_s, tok_e, tok_p, tok_o = [None] * 2, [None] * 2, [None] * 2, [None] * 2
                    for e in (0, 1):
                        hp = slice(e * HD, e * HD + HD)
                        pe.after(busy[e])
                        tok_s[e] = pe.do(m.mm(m.bank[4 + e][:, 0:W], b["q"][hp, i * P:W], b["k"][hp, 0:W]))
                    for e in (0, 1):
                        S, st = b["S"][:, e, 0:W], b["st"][:, e, :]
                        v.after(tok_s[e])
                        near = bs["bias"][:, bass.ds(pair * 2 + e, 1), T - W:T].rearrange("p o t -> p (o t)")
                        v.do(v.eng.tensor_tensor(S, m.bank[4 + e][:, 0:W], near, ALU.add))
                        v.after()
                        v.do(v.eng.tensor_tensor(S, S, sel[:, i, 0:W], ALU.add))
                        v.after()
                        v.do(v.eng.reduce_max(st[:, 0:1], S, AX))
                        v.after()
                        v.do(v.eng.tensor_scalar(st[:, 1:2], st[:, 0:1], -1.0, None, ALU.mult))
                        a.after(v.last)
                        tok_e[e] = a.do(a.eng.activation(b["E"][:, e, 0:W], S, ACT.Exp, bias=st[:, 1:2]))
                    for e in (0, 1):
                        pe.after(tok_e[e])
                        for k in range(i + 1):
                            ins = pe.eng.transpose(m.bank[6 + e][:, k * P:(k + 1) * P], b["E"][:, e, k * P:(k + 1) * P], m.c("ident"))
                        t = pe.do(ins)
                        a.after(t)
                        tok_p[e] = a.do(a.eng.copy(b["PT"][:, e, 0:W], m.bank[6 + e][:, 0:W]))
                    for e in (0, 1):
                        pe.after(tok_p[e])
                        for k in range(i + 1):
                            ins = m.mm(m.bank[4 + e][:, 0:HD + 1], b["PT"][:, e, k * P:(k + 1) * P], V[:, k, e, :], k == 0, k == i)
                        t = pe.do(ins)
                        v.after(t)
                        v.do(v.eng.reciprocal(b["st"][:, e, 2:3], m.bank[4 + e][:, HD:HD + 1]))
                        v.after()
                        busy[e] = v.do(v.eng.tensor_scalar(b["o"][:, i % 2, e * HD:(e + 1) * HD], m.bank[4 + e][:, 0:HD],
                                                           b["st"][:, e, 2:3], None, ALU.mult))
                    pe.after(busy[1])
                    t = pe.do(pe.eng.transpose(m.bank[6][:, 0:P], b["o"][:, i % 2, :], m.c("ident")))
                    a.after(t)
                    t = a.do(a.eng.copy(tile_of(mix, pair + 4, slice(i * P, W)), m.bank[6][:, 0:P]))
                    pe.after(t)
                m.join()


def block3(m):
    a, v, pe = m.act, m.dve, m.pe
    with m.buffers(mix=[KT, T]) as bm:
        with m.buffers(h=[KT, T], iw=[8 * TT]) as bh:
            m.iw = bh["iw"]
            with m.buffers(sq=[KT, T], rstd=[T]) as b:
                m.rms(m.x, bh["h"], "norm_mix_3", b["sq"], b["rstd"])
            mlstm(m, bh["h"], bm["mix"])
            dsa(m, bh["h"], bm["mix"])

        def add(j, k, t):
            v.after(t)
            v.do(v.eng.tensor_tensor(tile_of(m.x, k), tile_of(m.x, k), m.bank[2 * j][:], ALU.add), m.freed[j])

        m.pairs(m.tiles(bm["mix"]), KT, add)
    with m.buffers(h=[KT, T], act=[FT, T], raw=[4, T + 2], cv=[4, T], sq=[KT, T], rstd=[T]) as b:
        m.rms(m.x, b["h"], "norm_ffn_3", b["sq"], b["rstd"])
        v.after()
        v.do(v.eng.memset(b["raw"][:], 0.0))
        a.after(v.last)

        def gate(j, k, tg, tu):
            for part, t in ((0, tg), (1, tu)):
                n = 2 * j + part
                raw, cv = b["raw"][:, n, :], b["cv"][:, n, :]
                a.after(t)
                t = a.do(a.eng.copy(raw[:, 2:], m.bank[n][:]))
                c = k + FT * part
                v.after(t)
                v.do(v.eng.tensor_scalar(cv, raw[:, 0:T], m.col("ffn_conv_w_3", c), m.col("ffn_conv_b_3", c), ALU.mult, ALU.add))
                for tap in (1, 2):
                    v.after()
                    t = v.do(v.eng.scalar_tensor_tensor(cv, raw[:, tap:tap + T], m.col("ffn_conv_w_3", c + 2 * FT * tap), cv, ALU.mult, ALU.add))
                if part == 0:
                    a.after(t)
                    ts = a.do(a.eng.activation(cv, cv, ACT.Silu))
            v.after(ts)
            v.do(v.eng.tensor_tensor(tile_of(b["act"], k), b["cv"][:, 2 * j, :], b["cv"][:, 2 * j + 1, :], ALU.mult), m.freed[j])

        m.gated_pairs(b["h"], gate)
        m.join()
        m.down(b["act"], b["h"])
        m.join()
        for k in range(KT):
            v.after()
            v.do(v.eng.tensor_tensor(m.x[:, k, :], m.x[:, k, :], b["h"][:, k, :], ALU.add))
        m.rms(m.x, m.x, "norm_final_3", b["sq"], b["rstd"])
        m.join()


BLOCKS = (1, 2, 3)


def build(nc, adds_of, arrays_shapes, const_at, plan):
    dram = {k: nc.dram_tensor(f"in_{k}", s, F32, kind="ExternalInput").ap() for k, s in arrays_shapes.items()}
    out = nc.dram_tensor("out_x", (D, T), F32, kind="ExternalOutput").ap()
    m = Machine(nc, adds_of, dram, const_at, plan)
    for n, f in ((1, block1), (2, block2), (3, block3)):
        if n in BLOCKS:
            f(m)
    assert m.taken == len(plan), (m.taken, len(plan))
    m.join()
    done = m.dma(out.rearrange("(k p) t -> p k t", p=P), m.x[:], [e.last for e in m.compute if e.last])
    m.sp.wait(done)
    return {lp.index: lp.counted for lp in m.seen}


def lay_out(inputs, plan, const):
    flat = {k: np.asarray(v) for k, v in inputs.items()}
    flat["w_grp_a_2"] = flat["w_grp_a_2"].reshape(-1, 512) if "w_grp_a_2" in flat else None
    stream = np.zeros((len(plan), P, SLOT * P), np.float32)
    for s, slot in enumerate(plan):
        for n, block in enumerate(slot):
            for name, r, nr, c, nc_, part, *to in (block if isinstance(block, list) else [block]):
                a = flat[name]
                a = a[0] if a.ndim == 3 else a
                at = n * P + (to[0] if to else 0)
                stream[s, part:part + nr, at:at + nc_] = a[r:r + nr, c:c + nc_]
    at, n, want = column_plan()
    cols = np.zeros((n, P), np.float32)
    for name, k in want:
        if name in flat:
            a = flat[name].reshape(-1)
            if name == "idx_k_norm_3":
                a = np.concatenate([a, a])
            if k * P == a.size:
                cols[at[name]:at[name] + k] = a.reshape(k, P)
            else:
                full = np.zeros(k * P, np.float32)
                full[:a.size] = a
                cols[at[name]:at[name] + k] = full.reshape(k, P)
    out = {"x": np.ascontiguousarray(flat["x"].reshape(T, D).T), "cols": np.ascontiguousarray(cols.T), "const": const,
           "wstream": stream}
    if "rel_bias_3" in flat:
        out["rel_bias"] = np.zeros((P, 8), np.float32)
        out["rel_bias"][:32] = flat["rel_bias_3"]
    return out


def kernel(**inputs):
    import concourse.bacc as bacc
    from concourse.bass_utils import run_bass_kernel_spmd

    plan = weight_plan(BLOCKS)
    const, const_at = constants()
    arrays = lay_out(inputs, plan, const)
    shapes = {k: a.shape for k, a in arrays.items()}
    adds_of = build(bacc.Bacc("TRN2", target_bir_lowering=False, num_devices=1), {}, shapes, const_at, plan)
    nc = bacc.Bacc("TRN2", target_bir_lowering=False, num_devices=1)
    assert build(nc, adds_of, shapes, const_at, plan) == adds_of
    r = run_bass_kernel_spmd(nc, [{f"in_{k}": a for k, a in arrays.items()}], core_ids=[0])
    return np.ascontiguousarray(r.results[0]["out_x"].T).reshape(1, T, D)
```

```python
from contextlib import ExitStack, contextmanager
import math

import concourse.bass as bass
from concourse import mybir
from concourse.alu_op_type import AluOpType as ALU
import numpy as np

F32 = mybir.dt.float32
F32R = mybir.dt.float32r
ACT = mybir.ActivationFunctionType
AX = mybir.AxisListType.X

P = 128
T = 512
D = 1024
KT = D // P
TT = T // P
FF = 2816
FT = FF // P
HD = 64
NEG = -1e30
SLOT = 16
LC = 64
NCH = T // LC
LAM0 = 0.8 - 0.6 * math.exp(0.0)
LOG_DECAY = -math.exp(-0.5)
ALPHA = (2 * 2) ** 0.25
GROUPS = ((128, 1), (512, 4), (2048, 16))
TOPK = min(256, T // 4)
TAKEN = -3e38


class Loop:

    def __init__(self, index, trips, adds):
        self.index, self.trips, self.adds, self.reg, self.base = index, trips, adds, None, {}


class Token:

    def __init__(self, sem, n, loops):
        self.sem, self.n, self.loops = sem, n, tuple(loops)


class Count:

    def __init__(self, prog, name, start=None):
        self.prog, self.name, self.n = prog, name, 0
        self.sem = prog.nc.alloc_semaphore(name)
        if start is not None:
            start.sem_inc(self.sem, 1)
            self.n = 1
        prog.counts.append(self)

    def add(self, ins, k=1):
        ins.then_inc(self.sem, k)
        self.n += k
        return self.now()

    def now(self):
        return Token(self, self.n, self.prog.loops)


class Engine:

    def __init__(self, prog, eng, name, chained):
        self.prog, self.eng, self.name, self.chained = prog, eng, name, chained
        self.count = Count(prog, "done_" + name, eng)
        self.last = None
        self.pending = None

    def wait(self, token):
        if token is None:
            return
        value = token.n
        for loop in token.loops:
            step = loop.adds.get(token.sem.name, 0)
            if loop in self.prog.loops:
                if step:
                    value = value + loop.reg * step
            else:
                value = value + (loop.trips - 1) * step
        if isinstance(value, int) and value == 0:
            return
        self.eng.wait_ge(token.sem.sem, value)

    def after(self, *tokens):
        for t in tokens:
            self.wait(t)
        if self.chained:
            self.wait(self.pending)
            self.pending = None
        return self.eng

    def do(self, ins, count=None, k=1):
        self.last = self.pending = (count or self.count).add(ins, k)
        return self.last


class Program:

    def __init__(self, nc, adds_of):
        self.nc, self.adds_of, self.seen = nc, adds_of, []
        self.counts, self.loops = [], []
        self.pe = Engine(self, nc.tensor, "pe", False)
        self.act = Engine(self, nc.scalar, "act", True)
        self.dve = Engine(self, nc.vector, "dve", True)
        self.pool = Engine(self, nc.gpsimd, "pool", True)
        self.sp = Engine(self, nc.sync, "sp", False)
        self.compute = [self.pe, self.act, self.dve, self.pool]
        self.ndma = 0

    @contextmanager
    def loop(self, trips):
        for e in self.compute:
            if e.chained:
                e.after()
        lp = Loop(len(self.seen), trips, self.adds_of.get(len(self.seen), {}))
        self.seen.append(lp)
        lp.base = {c.name: c.n for c in self.counts}
        with self.nc.Fori(0, trips) as reg:
            lp.reg = reg
            self.loops.append(lp)
            yield reg
            for e in self.compute:
                if e.chained:
                    e.after()
            self.loops.pop()
        lp.counted = {c.name: c.n - lp.base.get(c.name, 0) for c in self.counts if c.n != lp.base.get(c.name, 0)}
        for c in self.counts:
            c.n += (trips - 1) * lp.adds.get(c.name, 0)

    def join(self):
        lasts = [(e, e.last) for e in self.compute]
        for e in self.compute:
            for o, last in lasts:
                if (o is not e or e.chained) and last is not None:
                    e.wait(last)
            e.pending = None

    def dma(self, out, in_, after=(), eng=None):
        e = eng or self.sp
        for t in after:
            e.wait(t)
        self.ndma += 1
        c = Count(self, f"moved_{self.ndma}")
        return c.add(e.eng.dma_start(out, in_), 16)


def weight_plan(blocks):
    plan = []

    def tiles(name, cols, kt=KT, row=0):
        return [(name, row + k * P, P, c, w, 0) for c, w in cols for k in range(kt)]

    def pairs(name, c0, n, kt=KT):
        for p in range(n // 2):
            plan.append(tiles(name, [(c0 + (2 * p + j) * P, P) for j in (0, 1)], kt))

    def gated(name_a, a0, name_b, b0, n):
        for p in range(n // 2):
            for name, c0 in ((name_a, a0), (name_b, b0)):
                plan.append(tiles(name, [(c0 + (2 * p + j) * P, P) for j in (0, 1)]))

    def down(name):
        for n in range(KT):
            for half in (0, 1):
                plan.append([(name, (half * FT // 2 + k) * P, P, n * P, P, 0) for k in range(FT // 2)])

    def qkv(name, q, k, v, n):
        for h in range(n):
            plan.append(tiles(name, [(q + h * P, P), (k + h * P, P)]))
            plan.append(tiles(name, [(v + h * P, P)]))

    if 1 in blocks:
        gated("ffn1_w_gate", 0, "ffn1_w_up", 0, FT)
        down("ffn1_w_down")
        qkv("w_in", 1824, 2336, 2848, 4)
        pairs("w_in", 0, 12)
        plan.append(tiles("w_in", [(1536, P), (1664, P)]))
        plan.append(tiles("w_in", [(1792, 32)]))
        plan.append([[("rwkv_w_up", 0, 64, c * P, P, 0), ("rwkv_a_up", 0, 64, c * P, P, 64)] for c in range(4)]
                    + [("rwkv_g_up", 0, P, c * P, P, 0) for c in range(4)]
                    + [("rwkv_g_up", P, 32, c * P, P, 0) for c in range(4)])
        pairs("w_o", 0, KT)
        gated("ffn2_w_gate", 0, "ffn2_w_up", 0, FT)
        down("ffn2_w_down")
    if 2 in blocks:
        for g in range(4):
            pairs("w_in_a_2", g * 512, 4)
            plan.append([("w_grp_a_2", g * 512 + k * P, P, n * P, P, 0) for n in range(4) for k in range(4)])
            pairs("w_in_a_2", 2048 + g * 512, 4)
        for n in range(KT):
            plan.append([("w_out_a_2", k * P, P, n * P, P, 0) for k in range(16)])
        for g in range(3):
            for h in range(8):
                c = g * D + h * P
                plan.append(tiles("w_in_b_2", [(c, P)]) + tiles("w_kv_2", [(c, P)]))
                plan.append(tiles("w_kv_2", [(3 * D + c, P)]))
        pairs("w_in_b_2", 3 * D, 8)
        pairs("w_out_b_2", 0, KT)
    if 3 in blocks:
        pairs("w_in_3", 0, 4)
        pairs("w_in_3", 512, 8)
        plan.append(tiles("w_in_3", [(1536, 4), (1540, 4)]))
        plan.append(tiles("w_in_3", [(3656, 8)]))
        plan.append([[("w_in_3", k * P, P, 3592, 64, 0), ("w_in_3", k * P, P, 3592, 64, 0, 64)]
                     for k in range(KT)])
        pairs("w_in_3", 3080, 4)
        qkv("w_in_3", 1544, 2056, 2568, 4)
        pairs("w_out_3", 0, KT)
        gated("w_up_3", 0, "w_up_3", FF, FT)
        down("w_down_3")
    return plan


def column_plan():
    want = [("ffn1_pre_g", 8), ("ffn1_post_g", 8), ("mix_pre_g", 8), ("mix_post_g", 8), ("shift_mu", 15),
            ("rwkv_w0", 4), ("rwkv_a0", 4), ("rwkv_k_k", 4), ("rwkv_k_a", 4), ("rwkv_r_k", 4), ("rwkv_gn_w", 4),
            ("rwkv_gn_b", 4), ("diff_lam_q1", 1), ("diff_lam_q2", 1), ("diff_lam_k1", 1), ("diff_lam_k2", 1),
            ("diff_subln_w", 1), ("ffn2_pre_g", 8), ("ffn2_post_g", 8), ("scale_a_2", 16), ("ln_g_2", 16),
            ("ln_b_2", 16), ("norm_mix_3", 8), ("mlstm_conv_w_3", 16), ("mlstm_conv_b_3", 4), ("i_bias_3", 1),
            ("f_bias_3", 1), ("mlstm_norm_3", 4), ("idx_k_norm_3", 1), ("norm_ffn_3", 8),
            ("ffn_conv_w_3", 132), ("ffn_conv_b_3", 44), ("norm_final_3", 8)]
    at, n = {}, 0
    for name, k in want:
        at[name] = n
        n += k
    return at, n, want


def permuted(tokens):
    return tokens.rearrange("p (m a r) -> p r a m", m=T // 16, a=4, r=4)


PASSING = ("reset", "pick", "bucket")


def constants():
    i = np.arange(P)
    c = {}
    c["ident"] = np.eye(P)
    c["ones"] = np.ones((P, P))
    c["headones"] = (i[:, None] // HD == i[None] // HD) * 1.0
    c["causal"] = np.where(i[None] <= i[:, None], 0.0, NEG)
    c["causal_t"] = np.where(i[:, None] <= i[None], 0.0, NEG)
    s, t = i[:, None] % LC, i[None] % LC
    c["pairmask"] = np.where(i[None] < LC, s < t, s <= t) * 1.0
    j = np.arange(LC)
    up, blk = j[:, None] < j[None], j[:, None] // 16 == j[None] // 16
    for name, m in (("near", up & blk), ("far", up & ~blk), ("near_t", up.T & blk)):
        z = np.zeros((P, LC))
        z[:LC] = m
        c[name] = z
    z = np.zeros((P, LC))
    z[:LC] = np.eye(LC)
    c["ident64"] = z
    c["reset"] = np.broadcast_to((np.arange(T) % LC != 0) * 1.0, (P, T))
    rel = P + i[:, None] - np.arange(2 * P)[None]
    c["dist0a"] = np.where(np.arange(2 * P)[None] < P, 1e30, np.where(rel >= 0, rel, 1e30))
    c["dist0"] = np.where((rel >= 0) & (rel <= GROUPS[0][0]), rel, 1e30)
    d = i[:, None] - i[None]
    tok = lambda q: 4 * (4 * (q % 32) + q // 32)
    dt = tok(i)[:, None] - tok(i)[None]
    c["dist1"] = np.where(dt >= 0, dt, 1e30)
    c["dist2"] = np.where((dt >= 0) & (i[:, None] // 32 == i[None] // 32), dt, 1e30)
    k = np.arange(1, 49, dtype=np.float32)
    sl = np.float32(2.0) ** (np.float32(-8.0) * k / np.float32(48))
    c["slopes"] = np.broadcast_to(-sl, (P, 48))
    c["early"] = np.broadcast_to(np.concatenate([w / np.minimum(np.arange(16) + 1, w) / w for w in (2, 4, 8, 16)]), (P, 64))
    z = np.zeros((P, 4 * P))
    for h in range(4):
        z[h, h * P:(h + 1) * P] = 1
    c["pick"] = z
    dist = np.maximum(T - 1 - np.arange(640), 0)
    large = 16 + np.floor(np.log(np.maximum(dist, 1) / 16.0) / math.log(8.0) * 16 + 1e-9).astype(int)
    bucket = np.where(dist < 16, dist, np.minimum(large, 31))
    c["anti"] = np.eye(P)[::-1]
    z = np.zeros((P, 640))
    z[:32] = bucket[None] == np.arange(32)[:, None]
    c["bucket"] = z
    at, n, parts = {}, 0, []
    for name, a in sorted(c.items(), key=lambda kv: kv[0] in PASSING):
        at[name] = (n, a.shape[1])
        n += a.shape[1]
        parts.append(a)
    return np.ascontiguousarray(np.concatenate(parts, 1).astype(np.float32)), at


class Pair:

    def __init__(self, hi, lo):
        self.hi, self.lo = hi, lo

    def __getitem__(self, key):
        return Pair(self.hi[key], self.lo[key])


class Machine(Program):

    def __init__(self, nc, adds_of, dram, const_at, plan):
        super().__init__(nc, adds_of)
        self.dram, self.plan = dram, plan
        self.col_at, self.ncols, _ = column_plan()
        self.const_at = const_at
        self.x = nc.alloc_sbuf_tensor("x", [P, KT, T], F32)
        self.cols = nc.alloc_sbuf_tensor("cols", [P, self.ncols], F32)
        resident = sum(w for name, (_, w) in const_at.items() if name not in PASSING)
        self.const = nc.alloc_sbuf_tensor("const", [P, resident], F32)
        self.slots = [nc.alloc_sbuf_tensor(f"slot{s}", [P, SLOT * P], F32) for s in (0, 1)]
        self.slot_hi = [nc.alloc_sbuf_tensor(f"slot_hi{s}", [P, SLOT * P], F32R) for s in (0, 1)]
        self.slot_lo = [nc.alloc_sbuf_tensor(f"slot_lo{s}", [P, SLOT * P], F32R) for s in (0, 1)]
        self.split_done = [Count(self, f"slot_split{s}", nc.gpsimd) for s in (0, 1)]
        self.bank = [nc.alloc_psum_tensor(f"bank{b}", [P, T], F32) for b in range(8)]
        self.loaded = [Count(self, f"slot_loaded{s}") for s in (0, 1)]
        self.slot_free = [Count(self, f"slot_free{s}", nc.tensor) for s in (0, 1)]
        self.freed = [Count(self, f"set_freed{s}", nc.vector) for s in (0, 1)]
        self.taken, self.toggle, self.primed = 0, 0, False
        self.slot_trips = []
        t = [self.dma(self.x[:], dram["x"].rearrange("(k p) t -> p k t", p=P)),
             self.dma(self.cols[:], dram["cols"]), self.dma(self.const[:], dram["const"][:, 0:resident])]
        for e in self.compute:
            e.after(*t)

    def c(self, name, a=0, b=None):
        n0, w = self.const_at[name]
        return self.const[:, n0 + a:n0 + (w if b is None else b)]

    def fetch(self, name, buf):
        n0, w = self.const_at[name]
        return self.dma(buf[:], self.dram["const"][:, n0:n0 + w], [e.last for e in self.compute if e.last], self.act)

    def col(self, name, k=0):
        k = k + self.col_at[name]
        return self.cols[:, k:k + 1] if isinstance(k, int) else self.cols[:, bass.ds(k, 1)]

    @contextmanager
    def buffers(self, split=(), **shapes):
        with ExitStack() as st:
            self.ndma += 1
            new = lambda k, v, dt: st.enter_context(self.nc.sbuf_tensor(f"{k}_{self.ndma}", [P, *v], dt))
            yield {k: tuple(new(f"{k}_{part}", v, F32R) for part in ("hi", "lo")) if k in split else new(k, v, F32)
                   for k, v in shapes.items()}
            self.join()

    def prefetch(self, ahead):
        s, first = self.toggle ^ ahead, self.taken + ahead
        index, uses = first, [first]
        for lp, step in zip(self.loops, self.slot_trips):
            index = index + lp.reg * step
            uses = range(first, first + lp.trips * step, step)
        nb = max([len(self.plan[u]) for u in uses if u < len(self.plan)], default=0)
        if nb == 0:
            return
        raw, hi, lo = (buf[s][:, 0:nb * P] for buf in (self.slots, self.slot_hi, self.slot_lo))
        self.sp.wait(self.split_done[s].now())
        src = self.dram["wstream"]
        src = src[index, :, 0:nb * P] if isinstance(index, int) else \
            src[bass.ds(index, 1), :, 0:nb * P].rearrange("o p n -> p (o n)")
        t = self.loaded[s].add(self.sp.eng.dma_start(raw, src), 16)
        a, g = self.act, self.pool
        a.after(t, self.slot_free[s].now())
        t = a.do(a.eng.copy(hi, raw))
        g.after(t)
        g.do(g.eng.tensor_tensor(lo, raw, hi.bitcast(F32), ALU.subtract), self.split_done[s])

    def take(self):
        if not self.primed:
            self.prefetch(0)
            self.primed = True
        s = self.toggle
        self.pe.after(self.split_done[s].now())
        self.prefetch(1)
        self.toggle, self.taken = 1 - s, self.taken + 1
        return s, Pair(self.slot_hi[s].rearrange("p (b n) -> p b n", n=P), self.slot_lo[s].rearrange("p (b n) -> p b n", n=P))

    @contextmanager
    def weight_loop(self, trips, slots):
        assert slots % 2 == 0
        first = self.taken
        with self.loop(trips) as i:
            self.slot_trips.append(slots)
            yield i
            self.slot_trips.pop()
            assert self.taken - first == slots, (self.taken - first, slots)
        for t in range(trips):
            for k in range(slots):
                assert len(self.plan[first + t * slots + k]) == len(self.plan[first + k])
        self.taken = first + trips * slots

    def mm(self, out, w, rhs, start=True, stop=True):
        return self.pe.eng.matmul(out, w, rhs, start=start, stop=stop, skip_group_check=True)

    def project(self, out, blocks, rhs, free=None, start=True, stop=True):
        for k, (b, r) in enumerate(zip(blocks, rhs)):
            self.mm(out, b.hi, r.hi, start and k == 0, False)
            self.mm(out, b.hi, r.lo, False, False)
            ins = self.mm(out, b.lo, r.hi, False, stop and k == len(blocks) - 1)
        return self.pe.do(ins, self.slot_free[free] if free is not None else None)

    def open_set(self, s, *tokens):
        self.pe.after(self.freed[s].now(), *tokens)

    def tiles(self, buf, n=KT):
        return [Pair(buf[0], buf[1])[:, k, :] for k in range(n)]

    def split(self, src, hi, lo, token=None):
        a, v = self.act, self.dve
        a.after(token)
        t = a.do(a.eng.copy(hi, src))
        v.after(t)
        return v.do(v.eng.tensor_tensor(lo, src, hi.bitcast(F32), ALU.subtract))

    def split_tiles(self, src, dst, n=KT, step=2):
        for k in range(0, n, step):
            q = slice(k, k + step)
            t = self.split(src[:, q, :], dst[0][:, q, :], dst[1][:, q, :], self.dve.last)
        self.pe.after(t)

    def moment(self, src, n, sq, out_bank, lhs, square=True):
        a, pe = self.act, self.pe
        used = []
        for k in range(n):
            if square:
                a.after(used[k - 2] if k >= 2 else None)
                t = a.do(a.eng.activation(sq[:, k % 2, :], src[:, k, :], ACT.Square))
                pe.after(t)
            ins = self.mm(out_bank, lhs, sq[:, k % 2, :] if square else src[:, k, :], k == 0, k == n - 1)
            used.append(pe.do(ins))
        return used[-1]

    def inv_root(self, out, ss, token, scale, eps, floor=None):
        v, a = self.dve, self.act
        v.after(token)
        if floor is None:
            t = v.do(v.eng.tensor_scalar(out, ss, scale, eps, ALU.mult, ALU.add))
        else:
            t = v.do(v.eng.tensor_scalar(out, ss, floor, None, ALU.max))
        a.after(t)
        t = a.do(a.eng.activation(out, out, ACT.Sqrt))
        v.after(t)
        return v.do(v.eng.reciprocal(out, out))

    def rms(self, src, dst, gain, b):
        sq, rstd = b["sq"], b["rstd"]
        self.join()
        t = self.moment(src, KT, sq, self.bank[7][:], self.c("ones"))
        self.inv_root(rstd[:], self.bank[7][:], t, 1.0 / D, 1e-6)
        v, parts = self.dve, isinstance(dst, tuple)
        for k in range(KT):
            out = sq[:, k % 2, :] if parts else dst[:, k, :]
            v.after()
            t = v.do(v.eng.scalar_tensor_tensor(out, src[:, k, :], self.col(gain, k), rstd[:], ALU.mult, ALU.mult))
            if parts:
                t = self.split(out, dst[0][:, k, :], dst[1][:, k, :], t)
        self.pe.after(t)
        return t

    def add_rms(self, y, gain, weight, b):
        self.rms(y, y, gain, b)
        v = self.dve
        for k in range(KT):
            v.after()
            v.do(v.eng.scalar_tensor_tensor(self.x[:, k, :], y[:, k, :], weight, self.x[:, k, :], ALU.mult, ALU.add))

    def gated_pairs(self, h, evacuate):
        with self.weight_loop(FT // 2, 2) as i:
            sg, g = self.take()
            tg = []
            for j in (0, 1):
                self.open_set(j)
                tg.append(self.project(self.bank[2 * j][:], [g[:, 8 * j + k, :] for k in range(KT)], self.tiles(h), sg if j else None))
            su, u = self.take()
            for j in (0, 1):
                tu = self.project(self.bank[2 * j + 1][:], [u[:, 8 * j + k, :] for k in range(KT)], self.tiles(h), su if j else None)
                evacuate(j, i * 2 + j, tg[j], tu)

    def down(self, act, y):
        half = FT // 2
        with self.weight_loop(KT // 2, 4) as i:
            for j in (0, 1):
                self.open_set(j)
                for part in (0, 1):
                    s, w = self.take()
                    t = self.project(self.bank[2 * j][:], [w[:, k, :] for k in range(half)],
                                     self.tiles(act, FT)[part * half:part * half + half], s, part == 0, part == 1)
                self.evacuate(y, i * 2 + j, j, t)

    def evacuate(self, dst, k, j, t):
        a = self.act
        a.after(t)
        out = dst[:, k, :] if isinstance(k, int) else dst[:, bass.ds(k, 1), :].rearrange("p o t -> p (o t)")
        return a.do(a.eng.copy(out, self.bank[2 * j][:]), self.freed[j])

    def pair_units(self, rhs, w, s, evac):
        n = len(rhs)
        for j in (0, 1):
            self.open_set(j)
            t = self.project(self.bank[2 * j][:], [w[:, n * j + k, :] for k in range(n)], rhs, s if j else None)
            evac(j, t)

    def pairs(self, rhs, n, evac):
        def body(i):
            for q in (0, 1):
                s, w = self.take()
                self.pair_units(rhs, w, s, lambda j, t: evac(j, i * 4 + 2 * q + j, t))

        if n == 4:
            body(0)
        else:
            with self.weight_loop(n // 4, 2) as i:
                body(i)


def tile_of(buf, k, cols=slice(None)):
    if isinstance(k, int):
        return buf[:, k, cols]
    return buf[:, bass.ds(k, 1), cols].rearrange("p o t -> p (o t)")


def store_split(m, j, src, dst, k, t):
    a, v = m.act, m.dve
    a.after(t)
    t = a.do(a.eng.copy(tile_of(dst[0], k), src))
    v.after(t)
    return v.do(v.eng.tensor_tensor(tile_of(dst[1], k), src, tile_of(dst[0], k).bitcast(F32), ALU.subtract), m.freed[j])


def swiglu_block(m, pre, post):
    with m.buffers(split=("act",), act=[FT, T]) as bo:
        with m.buffers(split=("h",), h=[KT, T], sg=[2, T], sq=[2, T], rstd=[T]) as b:
            m.rms(m.x, b["h"], pre, b)

            def gate(j, k, tg, tu):
                a, v = m.act, m.dve
                a.after(tg)
                t = a.do(a.eng.activation(b["sg"][:, j, :], m.bank[2 * j][:], ACT.Silu))
                v.after(t, tu)
                t = v.do(v.eng.tensor_tensor(b["sg"][:, j, :], b["sg"][:, j, :], m.bank[2 * j + 1][:], ALU.mult))
                store_split(m, j, b["sg"][:, j, :], bo["act"], k, t)

            m.gated_pairs(b["h"], gate)
        with m.buffers(y=[KT, T], sq=[2, T], rstd=[T]) as b:
            m.down(bo["act"], b["y"])
            m.add_rms(b["y"], post, 0.5, b)


def to_keys(m, src, dst, bank, tok, width=P):
    m.pe.after(tok)
    for k in range(TT):
        ins = m.pe.eng.transpose(bank[:, k * P:(k + 1) * P], src[:, k * P:(k + 1) * P], m.c("ident"))
    t = m.pe.do(ins)
    m.dve.after(t)
    return m.dve.do(m.dve.eng.tensor_copy(dst, bank[:].rearrange("p (k c) -> p k c", c=P) if width == P else
                                          bank[:].rearrange("p (k a c) -> p k a c", c=HD, a=2)))


def qkv_units(m, h, qT, kT, vT, order=lambda ap: ap):
    a, v = m.act, m.dve
    s, w = m.take()
    m.open_set(0)
    t = m.project(m.bank[0][:], [w[:, k, :] for k in range(KT)], m.tiles(h))
    a.after(t)
    tq = a.do(a.eng.mul(qT[:].rearrange("p (r a m) -> p r a m", r=4, a=4) if order is permuted else qT[:],
                        order(m.bank[0][:]), HD ** -0.5), m.freed[0])
    m.open_set(1)
    t = m.project(m.bank[2][:], [w[:, KT + k, :] for k in range(KT)], m.tiles(h), s)
    v.after(t)
    tk = v.do(v.eng.tensor_copy(kT[:].rearrange("p (r a m) -> p r a m", r=4, a=4) if order is permuted else kT[:],
                                order(m.bank[2][:])), m.freed[1])
    s, w = m.take()
    m.open_set(0)
    t = m.project(m.bank[0][:], [w[:, k, :] for k in range(KT)], m.tiles(h), s)
    a.after(t)
    tv = a.do(a.eng.copy(vT[:].rearrange("p (r a m) -> p r a m", r=4, a=4) if order is permuted else vT[:],
                         order(m.bank[0][:])), m.freed[0])
    return tq, tk, tv


def diff_attention(m, h, mix):
    a, v, pe = m.act, m.dve, m.pe
    with m.buffers(q=[T], k=[T], vT=[T], V=[TT, P], e=[2, T], pd=[T], pt=[TT, P], o=[T], sq=[1, T], rstd=[T], st=[16], lam=[8]) as b:
        lam = b["lam"]
        v.after()
        v.do(v.eng.tensor_tensor(lam[:, 0:2], m.cols[:, m.col_at["diff_lam_q1"]:m.col_at["diff_lam_q1"] + 2],
                                 m.cols[:, m.col_at["diff_lam_k1"]:m.col_at["diff_lam_k1"] + 2], ALU.mult))
        pe.after(v.last)
        t = pe.do(m.mm(m.bank[4][:, 0:2], m.c("ones"), lam[:, 0:2]))
        a.after(t)
        t = a.do(a.eng.activation(lam[:, 2:4], m.bank[4][:, 0:2], ACT.Exp))
        v.after(t)
        v.do(v.eng.tensor_tensor(lam[:, 4:5], lam[:, 3:4], lam[:, 2:3], ALU.subtract))
        v.after()
        v.do(v.eng.tensor_scalar(lam[:, 5:6], lam[:, 4:5], -LAM0, None, ALU.add))
        with m.weight_loop(4, 2) as head:
            tq, tk, tv = qkv_units(m, h, b["q"], b["k"], b["vT"])
            tV = to_keys(m, b["vT"], b["V"][:], m.bank[4], tv)
            pe.after(tq, tk, tV)
            st = b["st"]
            for i in range(TT):
                W = (i + 1) * P
                sb = [m.bank[4], m.bank[5]]
                ts = []
                if i:
                    pe.after(last_use)
                for c in (0, 1):
                    ts.append(pe.do(m.mm(sb[c][:, 0:W], b["q"][c * HD:(c + 1) * HD, i * P:W], b["k"][c * HD:(c + 1) * HD, 0:W])))
                for c in (0, 1):
                    v.after(ts[c])
                    v.do(v.eng.tensor_tensor(sb[c][:, i * P:W], sb[c][:, i * P:W], m.c("causal"), ALU.add))
                    v.after()
                    v.do(v.eng.reduce_max(st[:, c:c + 1], sb[c][:, 0:W], AX))
                    v.after()
                    t = v.do(v.eng.tensor_scalar(st[:, 2 + c:3 + c], st[:, c:c + 1], -1.0, None, ALU.mult))
                    a.after(t)
                    te = a.do(a.eng.activation(b["e"][:, c, 0:W], sb[c][:, 0:W], ACT.Exp, bias=st[:, 2 + c:3 + c],
                                               accum_out=st[:, 4 + c:5 + c]))
                last_use = te
                v.after(te)
                v.do(v.eng.reciprocal(st[:, 6:8], st[:, 4:6]))
                v.after()
                v.do(v.eng.tensor_tensor(st[:, 8:9], st[:, 7:8], lam[:, 5:6], ALU.mult))
                v.after()
                v.do(v.eng.tensor_scalar(b["pd"][:, 0:W], b["e"][:, 0, 0:W], st[:, 6:7], None, ALU.mult))
                v.after()
                t = v.do(v.eng.scalar_tensor_tensor(b["pd"][:, 0:W], b["e"][:, 1, 0:W], st[:, 8:9], b["pd"][:, 0:W], ALU.mult, ALU.add))
                pe.after(t)
                for k in range(i + 1):
                    ins = pe.eng.transpose(m.bank[6][:, k * P:(k + 1) * P], b["pd"][:, k * P:(k + 1) * P], m.c("ident"))
                t = pe.do(ins)
                v.after(t)
                t = v.do(v.eng.tensor_copy(b["pt"][:, 0:i + 1, :], m.bank[6][:, 0:W].rearrange("p (k c) -> p k c", c=P)))
                pe.after(t, tV)
                for k in range(i + 1):
                    ins = m.mm(m.bank[7][:, i * P:W], b["V"][:, k, :], b["pt"][:, k, :], k == 0, k == i)
                to = pe.do(ins)
            a.after(to)
            t = a.do(a.eng.copy(b["o"][:], m.bank[7][:]))
            a.after()
            t = a.do(a.eng.activation(b["sq"][:, 0, :], b["o"][:], ACT.Square))
            pe.after(t)
            t = pe.do(m.mm(m.bank[6][:], m.c("ones"), b["sq"][:, 0, :]))
            m.inv_root(b["rstd"][:], m.bank[6][:], t, 1.0 / P, 1e-5)
            v.after()
            v.do(v.eng.scalar_tensor_tensor(b["o"][:], b["o"][:], m.col("diff_subln_w"), b["rstd"][:], ALU.mult, ALU.mult))
            v.after()
            v.do(v.eng.tensor_scalar(tile_of(mix, head + 4), b["o"][:], 1.0 - LAM0, None, ALU.mult))
            m.join()


def rwkv_projections(m, h, b):
    a, v, pe = m.act, m.dve, m.pe
    v.after()
    v.do(v.eng.memset(b["raw"][:, :, 0:1], 0.0))
    v.after()
    v.do(v.eng.memset(b["lora"][:], 0.0))
    a.after(v.last)

    def shifted(j, k, t, dst, rows=P):
        raw, dif = b["raw"][0:rows, j, :], b["dif"][0:rows, j, :]
        a.after(t)
        t = a.do(a.eng.copy(raw[:, 1:T + 1], m.bank[2 * j][0:rows, :]))
        v.after(t)
        v.do(v.eng.tensor_tensor(dif, raw[:, 0:T], raw[:, 1:T + 1], ALU.subtract))
        v.after()
        return v.do(v.eng.scalar_tensor_tensor(dst[0:rows], dif, m.col("shift_mu", k)[0:rows], raw[:, 1:T + 1], ALU.mult, ALU.add), m.freed[j])

    m.pairs(m.tiles(h), 12, lambda j, k, t: shifted(j, k, t, tile_of(b["rkv"], k)))
    lora = b["lora"]
    s, w = m.take()
    m.pair_units(m.tiles(h), w, s, lambda j, t: shifted(j, 12 + j, t, lora[:, j, :]))
    s, w = m.take()
    m.open_set(0)
    t = m.project(m.bank[0][:], [w[:, k, :] for k in range(KT)], m.tiles(h), s)
    shifted(0, 14, t, lora[:, 2, :], 32)
    a.after(v.last)
    a.do(a.eng.activation(lora[0:64, 0, :], lora[0:64, 0, :], ACT.Tanh))
    a.after()
    tl = a.do(a.eng.activation(lora[:, 1:3, :], lora[:, 1:3, :], ACT.Sigmoid))
    m.join()


def rwkv_up(m, b):
    a, v, pe = m.act, m.dve, m.pe
    lora = b["lora"]
    m.split_tiles(lora, b["lora_parts"], 3, 3)
    up = Pair(*b["lora_parts"])
    s, w = m.take()
    for c in range(4):
        j = c % 2
        m.open_set(j)
        td = m.project(m.bank[2 * j][:], [w[0:64, c, :]], [up[0:64, 0, :]])
        ti = m.project(m.bank[2 * j + 1][:], [w[64:P, c, :]], [up[64:P, 0, :]])
        a.after(td)
        t = a.do(a.eng.activation(b["lw"][:, c, :], m.bank[2 * j][:], ACT.Sigmoid, bias=m.col("rwkv_w0", c)))
        v.after(t)
        v.do(v.eng.tensor_scalar(b["lw"][:, c, :], b["lw"][:, c, :], LOG_DECAY, None, ALU.mult))
        a.after(ti)
        a.do(a.eng.activation(b["iclr"][:, c, :], m.bank[2 * j + 1][:], ACT.Sigmoid, bias=m.col("rwkv_a0", c)), m.freed[j])
    for c in range(4):
        j = c % 2
        m.open_set(j)
        t = m.project(m.bank[2 * j][:], [w[:, 4 + c, :], w[0:32, 8 + c, :]], [up[:, 1, :], up[0:32, 2, :]], s if c == 3 else None)
        m.evacuate(b["gate"], c, j, t)


def rwkv_inputs(m, b):
    a, v, pe = m.act, m.dve, m.pe
    reset = b["lora"][:, 0, :]
    t_reset = m.fetch("reset", reset)
    r, k, kk = b["rkv"][:, 0:4, :], b["rkv"][:, 4:8, :], b["kk"]
    sq, rs = b["tmp"], b["rs"]
    for c in range(4):
        v.after()
        v.do(v.eng.tensor_scalar(kk[:, c, :], k[:, c, :], m.col("rwkv_k_k", c), None, ALU.mult))
    a.after(v.last)
    t = a.do(a.eng.activation(sq[:], kk[:], ACT.Square))
    pe.after(t)
    for c in range(4):
        t = pe.do(m.mm(m.bank[4 + c][:], m.c("headones"), sq[:, c, :]))
    for c in range(4):
        m.inv_root(rs[:, c, :], m.bank[4 + c][:], t, None, None, 1e-24)
    v.after()
    v.do(v.eng.tensor_tensor(kk[:], kk[:], rs[:], ALU.mult))
    for c in range(4):
        v.after()
        v.do(v.eng.tensor_scalar(sq[:, c, :], b["iclr"][:, c, :], -1.0, m.col("rwkv_k_a", c), ALU.add, ALU.mult))
        v.after()
        v.do(v.eng.scalar_tensor_tensor(k[:, c, :], sq[:, c, :], 1.0, k[:, c, :], ALU.add, ALU.mult))
    for c in range(4):
        v.after()
        v.do(v.eng.scalar_tensor_tensor(sq[:, c, :], r[:, c, :], m.col("rwkv_r_k", c), k[:, c, :], ALU.mult, ALU.mult))
    pe.after(v.last)
    for c in range(4):
        t = pe.do(m.mm(m.bank[4 + c][:], m.c("headones"), sq[:, c, :]))
    for c in range(4):
        v.after(t)
        v.do(v.eng.tensor_tensor(b["bonus"][:, c, :], m.bank[4 + c][:], b["rkv"][:, 8 + c, :], ALU.mult))
    cum = b["tmp"]
    v.after(t_reset)
    for c in range(4):
        v.after()
        v.do(v.eng.tensor_tensor_scan(cum[:, c, :], reset, b["lw"][:, c, :], 0.0, ALU.mult, ALU.add))
    ch = lambda ap: ap.rearrange("p c (n l) -> p c n l", l=LC)
    a.after(v.last)
    tp = a.do(a.eng.activation(rs[:], cum[:], ACT.Exp))
    a.after()
    v.after()
    v.do(v.eng.tensor_tensor(b["lw"][:], cum[:], b["lw"][:], ALU.subtract))
    a.after(v.last)
    tx = a.do(a.eng.activation(b["lw"][:], b["lw"][:], ACT.Exp))
    v.after(tp)
    v.do(v.eng.tensor_copy(b["plast"][:], ch(rs[:])[:, :, :, LC - 1]))
    AR, BK = b["AR"], b["BK"]
    for c in range(4):
        one = lambda ap: ap[:, c, :].rearrange("p (n l) -> p n l", l=LC)
        v.after()
        v.do(v.eng.tensor_tensor(AR[:, c, :, LC:P], one(r), one(rs), ALU.mult))
        v.after(tx)
        v.do(v.eng.scalar_tensor_tensor(AR[:, c, :, 0:LC], one(kk), -1.0, one(b["lw"]), ALU.mult, ALU.mult))
    a.after(v.last)
    ti = a.do(a.eng.activation(rs[:], cum[:], ACT.Exp, scale=-1.0))
    v.after(ti)
    for c in range(4):
        one = lambda ap: ap[:, c, :].rearrange("p (n l) -> p n l", l=LC)
        v.after()
        v.do(v.eng.tensor_tensor(BK[:, c, :, LC:P], one(k), one(rs), ALU.mult))
        v.after()
        v.do(v.eng.tensor_tensor(kk[:, c, :], kk[:, c, :], b["iclr"][:, c, :], ALU.mult))
        v.after()
        v.do(v.eng.tensor_tensor(BK[:, c, :, 0:LC], one(kk), one(rs), ALU.mult))
    m.join()


def rwkv_chunks(m, b, yT):
    a, v, pe = m.act, m.dve, m.pe
    H8 = lambda bank: bank[0:LC, :].rearrange("p (h n) -> p h n", n=LC)
    bc = lambda name, n=8: m.c(name)[0:LC, :].unsqueeze(1).broadcast_to([LC, n, LC])
    v.after()
    v.do(v.eng.memset(b["X"][:], 0.0))
    v.after()
    v.do(v.eng.memset(b["vs"][:], 0.0))
    v.after()
    v.do(v.eng.memset(b["y"][:], 0.0))
    pe.after(v.last)
    a.after(v.last)
    B = m.bank
    place = lambda hd: hd % 2 * 4 + hd // 2
    with m.loop(NCH) as ci:
        ar, bk, vs = b["ar"], b["bk"], b["vs"]
        pick = lambda buf: buf[:, :, bass.ds(ci, 1), :].rearrange("p c o n -> p c (o n)")
        v.after()
        t_ar = v.do(v.eng.tensor_copy(ar[:], pick(b["AR"])))
        a.after()
        t_bk = a.do(a.eng.copy(bk[:], pick(b["BK"])))
        a.after()
        t_vs = a.do(a.eng.copy(vs[:, :, LC:P], b["rkv"][:, 8:12, bass.ds(ci * LC, LC)]))
        pe.after(t_ar, t_bk)
        for o in range(8):
            q = slice(o // 4 * HD, o // 4 * HD + HD)
            ins = m.mm(B[o // 4][:, (o % 4) * P:(o % 4 + 1) * P], bk[q, o % 4, :], ar[q, o % 4, :])
            if o % 4 == 3:
                t = pe.do(ins)
                v.after(t)
                v.do(v.eng.tensor_tensor(b["G"][:, o - 3:o + 1, :], B[o // 4][:].rearrange("p (h n) -> p h n", n=P),
                                         m.c("pairmask").unsqueeze(1).broadcast_to([P, 4, P]), ALU.mult))
        for o in range(8):
            q = slice(o // 4 * HD, o // 4 * HD + HD)
            ins = m.mm(B[(2, 5)[o // 4]][0:LC, (o % 4) * LC:(o % 4 + 1) * LC], ar[q, o % 4, 0:LC], bk[q, o % 4, 0:LC])
        tn = pe.do(ins)
        for c in range(4):
            ins = pe.eng.transpose(B[3][:, c * P:(c + 1) * P], bk[:, c, :], m.c("ident"))
        t = pe.do(ins)
        a.after(t)
        t_bkt = a.do(a.eng.copy(b["bkt"][:], B[3][:]))
        pe.after(t_vs)
        for c in range(4):
            ins = pe.eng.transpose(B[4][:, c * P:(c + 1) * P], vs[:, c, :], m.c("ident"))
        t = pe.do(ins)
        a.after(t)
        t_v = a.do(a.eng.copy(b["UV"][LC:P, :], B[4][LC:P, :]))
        N, NT, W, WT = b["N"], b["NT"], b["W"], b["WT"]
        near, near_t, far = b["near"], b["near_t"], b["far"]
        v.after(tn)
        for e, bank in enumerate((B[2], B[5])):
            half = bank[0:LC, 0:4 * LC].rearrange("p (h n) -> p h n", n=LC)
            v.after()
            v.do(v.eng.tensor_tensor(near_t[0:LC, 4 * e:4 * e + 4, :], half, bc("near_t", 4), ALU.mult))
        n_of = b["G"][0:LC, :, 0:LC]
        v.after()
        v.do(v.eng.tensor_tensor(near[0:LC], n_of, bc("near"), ALU.mult))
        v.after()
        v.do(v.eng.tensor_tensor(far[0:LC], n_of, bc("far"), ALU.mult))
        v.after()
        v.do(v.eng.tensor_tensor(W[0:LC], near[0:LC], bc("ident64"), ALU.add))
        v.after()
        v.do(v.eng.tensor_tensor(WT[0:LC], near_t[0:LC], bc("ident64"), ALU.add))

        def product(bank, lhs, rhs, *tokens):
            pe.after(*tokens)
            m.mm(bank[:, 0:2], m.c("ident"), m.c("ident", 0, 2))
            for hd in range(8):
                ins = m.mm(bank[0:LC, hd * LC:(hd + 1) * LC], lhs[0:LC, hd, :], rhs[0:LC, hd, :])
            return pe.do(ins)

        cur, cur_t, ready = near, near_t, v.last
        for step in range(3):
            nxt, nxt_t = (N, NT) if step % 2 == 0 else (near, near_t)
            t1 = product(B[5], cur_t, cur, ready)
            t2 = product(B[6], cur, cur_t)
            a.after(t1)
            ta = a.do(a.eng.copy(nxt[0:LC], H8(B[5])))
            v.after(t2)
            tb = v.do(v.eng.tensor_copy(nxt_t[0:LC], H8(B[6])))
            t1 = product(B[7], nxt_t, W, ta, tb)
            t2 = product(B[2], nxt, WT)
            v.after(t1)
            v.do(v.eng.tensor_tensor(W[0:LC], H8(B[7]), W[0:LC], ALU.add))
            v.after(t2)
            ready = v.do(v.eng.tensor_tensor(WT[0:LC], H8(B[2]), WT[0:LC], ALU.add))
            cur, cur_t = nxt, nxt_t
        E, ET, E2T = b["near"], b["near_t"], b["N"]
        t1 = product(B[5], WT, far, ready)
        t2 = product(B[6], far, WT)
        a.after(t1)
        ta = a.do(a.eng.copy(E[0:LC], H8(B[5])))
        v.after(t2)
        tb = v.do(v.eng.tensor_copy(ET[0:LC], H8(B[6])))
        t1 = product(B[7], E, ET, ta, tb)
        a.after(t1)
        ta = a.do(a.eng.copy(E2T[0:LC], H8(B[7])))
        t1 = product(B[5], E2T, W, ta)
        v.after(t1)
        tb = v.do(v.eng.tensor_tensor(W[0:LC], H8(B[5]), W[0:LC], ALU.add))
        t1 = product(B[6], ET, W, tb)
        v.after(t1)
        t_w = v.do(v.eng.tensor_tensor(W[0:LC], H8(B[6]), W[0:LC], ALU.add))
        X, UV, G = b["X"], b["UV"], b["G"]
        pe.after(t_v, t_w)
        for c in range(4):
            m.mm(B[0][0:LC, c * P:(c + 1) * P], ar[:, c, 0:LC], X[:, c, :], True, False)
            for hd in (2 * c, 2 * c + 1):
                ins = m.mm(B[0][0:LC, hd * LC:(hd + 1) * LC], G[LC:P, place(hd), 0:LC], UV[LC:P, hd * LC:(hd + 1) * LC], False, hd % 2 == 1)
        t = pe.do(ins)
        v.after(t)
        t = v.do(v.eng.tensor_copy(b["Z"][0:LC].rearrange("p (e c) n -> p c e n", e=2), B[0][0:LC, :].rearrange("p (c e n) -> p c e n", e=2, n=LC)))
        t = product(B[1], W, b["Z"], t)
        v.after(t)
        t_u = v.do(v.eng.tensor_copy(UV[0:LC, :].rearrange("p (c e n) -> p c e n", e=2, n=LC), B[1][0:LC, :].rearrange("p (e c n) -> p c e n", e=2, n=LC)))
        pe.after(t_u, t_bkt)
        for c in range(4):
            m.mm(B[2][0:LC, c * P:(c + 1) * P], ar[:, c, LC:P], X[:, c, :], True, False)
            for hd in (2 * c, 2 * c + 1):
                ins = m.mm(B[2][0:LC, hd * LC:(hd + 1) * LC], G[:, place(hd), LC:P], UV[:, hd * LC:(hd + 1) * LC], False, hd % 2 == 1)
        t_y = pe.do(ins)
        for c in range(4):
            ins = m.mm(B[3][:, c * P:(c + 1) * P], b["bkt"][:, c * P:(c + 1) * P], UV[:, c * P:(c + 1) * P])
        t_x = pe.do(ins)
        a.after(t_y)
        t_ys = a.do(a.eng.copy(b["y"][0:LC, :], B[2][0:LC, :]))
        v.after(t_x)
        v.do(v.eng.tensor_tensor(X[:], B[3][:].rearrange("p (c n) -> p c n", n=P), X[:], ALU.add))
        v.after()
        v.do(v.eng.tensor_tensor(X[:], X[:], m.c("headones").unsqueeze(1).broadcast_to([P, 4, P]), ALU.mult))
        for c in range(4):
            v.after()
            v.do(v.eng.tensor_scalar(X[:, c, :], X[:, c, :],
                                     b["plast"][:, c, bass.ds(ci, 1)], None, ALU.mult))
        pe.after(t_ys)
        for c in range(4):
            ins = pe.eng.transpose(B[4][:, c * P:(c + 1) * P], b["y"][:, c * P:(c + 1) * P], m.c("ident"))
        t = pe.do(ins)
        a.after(t)
        a.do(a.eng.copy(yT[:, :, bass.ds(ci * LC, LC)], B[4][:].rearrange("p (c l) -> p c l", l=P)[:, :, 0:LC]))
        m.join()


def rwkv(m, bo, mix):
    a, v, pe = m.act, m.dve, m.pe
    with m.buffers(gate=[4, T], bonus=[4, T], AR=[4, NCH, P], BK=[4, NCH, P], plast=[4, NCH]) as b:
        b = {**b, **bo}
        with m.buffers(lw=[4, T], iclr=[4, T]) as b2:
            with m.buffers(split=("lora_parts",), lora_parts=[3, T]) as b3:
                rwkv_up(m, {**b, **b2, **b3})
            with m.buffers(kk=[4, T], tmp=[4, T], rs=[4, T]) as b3:
                rwkv_inputs(m, {**b, **b2, **b3})
        with m.buffers(yT=[4, T], X=[4, P], ar=[4, P], bk=[4, P], vs=[4, P], G=[8, P], bkt=[T], UV=[T], N=[8, LC], NT=[8, LC],
                       W=[8, LC], WT=[8, LC], near=[8, LC], near_t=[8, LC], far=[8, LC], Z=[8, LC]) as b3:
            yT, b["y"] = b3["yT"], b["lora"][:, 1, :]
            rwkv_chunks(m, {**b, **b3}, yT)
            flat = lambda buf: buf.rearrange("p c n l -> p (c n l)")
            dev, sq = (flat(b["AR"])[:, n * 4 * T:(n + 1) * 4 * T].rearrange("p (c t) -> p c t", t=T) for n in (0, 1))
            rs = flat(b["BK"])[:, 0:4 * T].rearrange("p (c t) -> p c t", t=T)
            for c in range(4):
                t = pe.do(m.mm(m.bank[4 + c][:], m.c("headones"), yT[:, c, :]))
            for c in range(4):
                v.after(t)
                v.do(v.eng.scalar_tensor_tensor(dev[:, c, :], m.bank[4 + c][:], -1.0 / HD, yT[:, c, :], ALU.mult, ALU.add))
            a.after(v.last)
            t = a.do(a.eng.activation(sq[:], dev[:], ACT.Square))
            pe.after(t)
            for c in range(4):
                t = pe.do(m.mm(m.bank[4 + c][:], m.c("headones"), sq[:, c, :]))
            for c in range(4):
                m.inv_root(rs[:, c, :], m.bank[4 + c][:], t, 1.0 / HD, 64e-5)
            for c in range(4):
                v.after()
                v.do(v.eng.scalar_tensor_tensor(dev[:, c, :], dev[:, c, :], m.col("rwkv_gn_w", c), rs[:, c, :], ALU.mult, ALU.mult))
                v.after()
                v.do(v.eng.scalar_tensor_tensor(dev[:, c, :], dev[:, c, :], m.col("rwkv_gn_b", c), b["bonus"][:, c, :], ALU.add, ALU.add))
            v.after()
            v.do(v.eng.tensor_tensor(mix[:, 0:4, :], dev[:], b["gate"][:], ALU.mult))
            m.join()


def block1(m):
    swiglu_block(m, "ffn1_pre_g", "ffn1_post_g")
    with m.buffers(mix=[KT, T]) as bm:
        with m.buffers(rkv=[12, T], lora=[3, T]) as br:
            with m.buffers(split=("h",), h=[KT, T]) as bh:
                with m.buffers(sq=[2, T], rstd=[T]) as b:
                    m.rms(m.x, bh["h"], "mix_pre_g", b)
                diff_attention(m, bh["h"], bm["mix"])
                with m.buffers(raw=[2, T + 1], dif=[2, T]) as b:
                    rwkv_projections(m, bh["h"], {**br, **b})
            rwkv(m, br, bm["mix"])
        with m.buffers(y=[KT, T], sq=[2, T], rstd=[T]) as b:
            project_out(m, bm["mix"], lambda j, k, t: m.evacuate(b["y"], k, j, t))
            m.add_rms(b["y"], "mix_post_g", 1.0, b)
    swiglu_block(m, "ffn2_pre_g", "ffn2_post_g")


def project_out(m, src, evac):
    with m.buffers(split=("parts",), parts=[KT, T]) as b:
        m.split_tiles(src, b["parts"])
        m.pairs(m.tiles(b["parts"]), KT, evac)


def pool_gated(m, act):
    a, v, pe = m.act, m.dve, m.pe
    PAD = 16
    with m.buffers(split=("pooled", "xs"), xs=[KT, T], u=[2, PAD + T], wa=[PAD + T], wb=[PAD + T], mean=[T], pooled=[4, T],
                   mixed=[4, T], sg=[2, T]) as b:
        v.after()
        v.do(v.eng.memset(b["u"][:], 0.0))
        a.after(v.last)
        m.split_tiles(m.x, b["xs"])
        xs = m.tiles(b["xs"])
        for g, w in enumerate((2, 4, 8, 16)):
            def window(j, k, t):
                u = b["u"][:, j, :]
                a.after(t)
                t = a.do(a.eng.copy(u[:, PAD:], m.bank[2 * j][:]))
                cur, step, n = u, 1, 0
                v.after(t)
                while step < w:
                    nxt = (b["wa"], b["wb"])[n % 2][:]
                    lo = 2 * step - 1
                    v.after()
                    v.do(v.eng.tensor_tensor(nxt[:, lo:], cur[:, lo:], cur[:, lo - step:PAD + T - step], ALU.add))
                    cur, step, n = nxt, 2 * step, n + 1
                v.after()
                v.do(v.eng.scalar_tensor_tensor(b["mean"][:, PAD:], cur[:, 2 * PAD:], 1.0 / w, u[:, 2 * PAD:], ALU.mult, ALU.subtract))
                v.after()
                v.do(v.eng.tensor_tensor(cur[:, PAD:2 * PAD], cur[:, PAD:2 * PAD], m.c("early", 16 * g, 16 * g + 16), ALU.mult))
                v.after()
                t = v.do(v.eng.tensor_tensor(b["mean"][:, 0:PAD], cur[:, PAD:2 * PAD], u[:, PAD:2 * PAD], ALU.subtract))
                store_split(m, j, b["mean"][:], b["pooled"], k, t)

            m.pairs(xs, 4, window)
            pe.after(v.last)
            s, wg = m.take()
            for k in range(4):
                j = k % 2
                m.open_set(j)
                t = m.project(m.bank[2 * j][:], [wg[:, 4 * k + c, :] for c in range(4)], m.tiles(b["pooled"], 4), s if k == 3 else None)
                a.after(t)
                a.do(a.eng.activation(b["mixed"][:, k, :], m.bank[2 * j][:], ACT.Copy, scale=m.col("scale_a_2", 4 * g + k)), m.freed[j])
            t_mixed = a.last

            def gate(j, k, t):
                a.after(t)
                t = a.do(a.eng.activation(b["sg"][:, j, :], m.bank[2 * j][:], ACT.Silu))
                v.after(t, t_mixed)
                t = v.do(v.eng.tensor_tensor(b["sg"][:, j, :], b["sg"][:, j, :], b["mixed"][:, k, :], ALU.mult))
                store_split(m, j, b["sg"][:, j, :], act, 4 * g + k, t)

            m.pairs(xs, 4, gate)
            a.after(v.last)


def layer_norm(m, y, l, b):
    sq, rstd = b["sq"], b["rstd"]
    v, a, pe = m.dve, m.act, m.pe
    m.join()
    for k in range(KT):
        v.after()
        v.do(v.eng.scalar_tensor_tensor(y[:, k, :], m.x[:, k, :], ALPHA, y[:, k, :], ALU.mult, ALU.add))
    pe.after(v.last)
    t = m.moment(y, KT, None, m.bank[6][:], m.c("ones"), square=False)
    v.after(t)
    v.do(v.eng.tensor_scalar(rstd[:], m.bank[6][:], 1.0 / D, None, ALU.mult))
    for k in range(KT):
        v.after()
        v.do(v.eng.tensor_tensor(y[:, k, :], y[:, k, :], rstd[:], ALU.subtract))
    a.after(v.last)
    t = m.moment(y, KT, sq, m.bank[7][:], m.c("ones"))
    m.inv_root(rstd[:], m.bank[7][:], t, 1.0 / D, 1e-5)
    for k in range(KT):
        v.after()
        v.do(v.eng.scalar_tensor_tensor(y[:, k, :], y[:, k, :], m.col("ln_g_2", 8 * l + k), rstd[:], ALU.mult, ALU.mult))
        v.after()
        v.do(v.eng.tensor_scalar(m.x[:, k, :], y[:, k, :], m.col("ln_b_2", 8 * l + k), None, ALU.add))
    m.join()


def values_with_ones(m, b, tv):
    return to_keys(m, b["vT"], b["V"].rearrange("p k (a c) -> p k a c", a=2)[:, :, :, 0:HD], m.bank[6], tv, HD)


def dilated_group(m, xs, g, b, O):
    a, v, pe = m.act, m.dve, m.pe
    nt, kw = (2, 2 * P) if g == 0 else (4, P)
    V = b["V"].rearrange("p k (a c) -> p k a c", a=2)
    with m.weight_loop(8, 2) as pair:
        tq, tk, tv = qkv_units(m, xs, b["q"], b["k"], b["vT"], (lambda ap: ap) if g == 0 else permuted)
        tV = values_with_ones(m, b, tv)
        pe.after(tq, tk, tV)
        busy = [None, None]
        for first in range(0, TT, nt):
            tok_s, tok_e, tok_p = [None, None], [None, None], [None, None]
            for e in (0, 1):
                hp = slice(e * HD, e * HD + HD)
                pe.after(busy[e])
                for n in range(nt):
                    i = first + n
                    if g == 0 and i == 0:
                        m.mm(m.bank[4 + e][:, 0:P], b["q"][hp, 0:P], b["k"][hp, 0:P])
                        ins = m.mm(m.bank[4 + e][:, P:2 * P], b["q"][hp, 0:P], b["k"][hp, 0:P])
                    else:
                        keys = slice((i - 1) * P, (i + 1) * P) if g == 0 else slice(i * P, (i + 1) * P)
                        ins = m.mm(m.bank[4 + e][:, n * kw:(n + 1) * kw], b["q"][hp, i * P:(i + 1) * P], b["k"][hp, keys])
                tok_s[e] = pe.do(ins)
            for e in (0, 1):
                S, st = b["S"][:, e, :].rearrange("p (n k) -> p n k", k=kw), b["st"][:, e, :]
                n0, _ = m.const_at["slopes"]
                slope = m.const[:, bass.ds(pair * 2 + (n0 + 16 * g + e), 1)]
                if g == 0 and first == 0:
                    n1, _ = m.const_at["dist0a"]
                    dist = m.const[:, n1:n1 + 4 * P].rearrange("p (n k) -> p n k", k=kw)
                else:
                    dist = m.c(f"dist{g}").unsqueeze(1).broadcast_to([P, nt, kw])
                score = m.bank[4 + e].rearrange("p (n k) -> p n k", k=kw)
                v.after(tok_s[e])
                v.do(v.eng.scalar_tensor_tensor(S, dist, slope, score, ALU.mult, ALU.add))
                v.after()
                v.do(v.eng.reduce_max(st[:, 0:nt], S, AX))
                v.after()
                v.do(v.eng.tensor_tensor(S, S, st[:, 0:nt].unsqueeze(2).broadcast_to([P, nt, kw]), ALU.subtract))
                a.after(v.last)
                tok_e[e] = a.do(a.eng.activation(b["E"][:, e, :], b["S"][:, e, :], ACT.Exp))
                v.after()
                v.do(v.eng.tensor_copy(O[:, first:first + nt, bass.ds(pair * 2 + e, 1), HD + 1:HD + 2].rearrange("p n o c -> p n (o c)"),
                                       st[:, 0:nt].unsqueeze(2)))
            for e in (0, 1):
                pe.after(tok_e[e])
                for k in range(4):
                    ins = pe.eng.transpose(m.bank[6 + e][:, k * P:(k + 1) * P], b["E"][:, e, k * P:(k + 1) * P], m.c("ident"))
                t = pe.do(ins)
                a.after(t)
                tok_p[e] = a.do(a.eng.copy(b["PT"][:, e, :], m.bank[6 + e][:]))
            for e in (0, 1):
                pe.after(tok_p[e])
                for n in range(nt):
                    i = first + n
                    out = m.bank[4 + e][:, n * (HD + 1):(n + 1) * (HD + 1)]
                    blocks = [(n, i)] if g else [(2 * n, i - 1), (2 * n + 1, i)][i == 0:]
                    for z, (blk, key) in enumerate(blocks):
                        ins = m.mm(out, b["PT"][:, e, blk * P:(blk + 1) * P], V[:, key, e, :], z == 0, z == len(blocks) - 1)
                t = pe.do(ins)
                v.after(t)
                busy[e] = v.do(v.eng.tensor_copy(O[:, first:first + nt, bass.ds(pair * 2 + e, 1), 0:HD + 1].rearrange("p n o c -> p n (o c)"),
                                                 m.bank[4 + e][:, 0:nt * (HD + 1)].rearrange("p (n c) -> p n c", c=HD + 1)))
        m.join()


def dilated_groups(m, bo, gate):
    a, v = m.act, m.dve
    natural = m.nc.dram_tensor("group0_natural", (T, 16 * (HD + 2)), F32, kind="Internal").ap()
    with m.buffers(split=("xs",), xs=[KT, T]) as bx:
        xs = bx["xs"]
        m.split_tiles(m.x, xs)
        with m.buffers(q=[T], k=[T], vT=[T], V=[TT, 2 * (HD + 1)], S=[2, T], E=[2, T], PT=[2, T], st=[2, 4]) as b:
            v.after()
            v.do(v.eng.memset(b["V"][:], 1.0))
            dilated_group(m, xs, 0, b, bo["O0"])
            rows = lambda buf: buf.rearrange("p n h c -> p n (h c)")
            out = m.dma(natural.rearrange("(n p) c -> p n c", p=P), rows(bo["O0"]), [v.last], m.act)
            back = natural.rearrange("(m a r) c -> a m r c", a=4, r=4)
            back_at = [m.dma(rows(bo["O0"])[32 * k:32 * k + 32], back[k], [out], m.act) for k in range(4)]
            dilated_group(m, xs, 1, b, bo["O1"])
            dilated_group(m, xs, 2, b, bo["O2"])

        def evacuate(j, k, t):
            a.after(t)
            a.do(a.eng.activation(tile_of(gate, k), m.bank[2 * j][:], ACT.Silu), m.freed[j])

        m.pairs(m.tiles(xs), KT, evacuate)
    return back_at


def merge_groups(m, bo, gate, back_at):
    a, v, pe = m.act, m.dve, m.pe
    with m.buffers(top=[64], w=[3, 64], rec=[64], merged=[64, HD]) as b:
        O = [bo[f"O{g}"].rearrange("p n h c -> p (n h) c") for g in range(3)]
        v.after(*back_at)
        v.do(v.eng.tensor_tensor(b["top"][:], O[0][:, :, HD + 1], O[1][:, :, HD + 1], ALU.max))
        v.after()
        v.do(v.eng.tensor_tensor(b["top"][:], b["top"][:], O[2][:, :, HD + 1], ALU.max))
        for g in range(3):
            v.after()
            v.do(v.eng.tensor_tensor(b["w"][:, g, :], O[g][:, :, HD + 1], b["top"][:], ALU.subtract))
        a.after(v.last)
        t = a.do(a.eng.activation(b["w"][:], b["w"][:], ACT.Exp))
        v.after(t)
        for g in range(3):
            v.after()
            v.do(v.eng.tensor_tensor(O[g][:, :, 0:HD + 1], O[g][:, :, 0:HD + 1], b["w"][:, g, :].unsqueeze(2).broadcast_to([P, 64, HD + 1]), ALU.mult))
        for g in (1, 2):
            v.after()
            v.do(v.eng.tensor_tensor(O[0][:, :, 0:HD + 1], O[0][:, :, 0:HD + 1], O[g][:, :, 0:HD + 1], ALU.add))
        v.after()
        v.do(v.eng.reciprocal(b["rec"][:], O[0][:, :, HD]))
        v.after()
        t = v.do(v.eng.tensor_tensor(b["merged"][:], O[0][:, :, 0:HD], b["rec"][:].unsqueeze(2).broadcast_to([P, 64, HD]), ALU.mult))
        rows = b["merged"].rearrange("p (n h) c -> p n (h c)", n=TT)
        m.join()
        read = []
        for c in range(KT):
            bank = m.bank[4 + c % 4]
            pe.after(read[c - 4] if c >= 4 else None)
            for n in range(TT):
                ins = pe.eng.transpose(bank[:, n * P:(n + 1) * P], rows[:, n, c * P:(c + 1) * P], m.c("ident"))
            t = pe.do(ins)
            v.after(t)
            read.append(v.do(v.eng.tensor_tensor(permuted(gate[:, c, :]), bank[:].rearrange("p (r a m) -> p r a m", r=4, a=4),
                                                 permuted(gate[:, c, :]), ALU.mult)))


def dilated_mixer(m):
    with m.buffers(gate=[KT, T]) as bg:
        with m.buffers(O0=[TT, 16, HD + 2], O1=[TT, 16, HD + 2], O2=[TT, 16, HD + 2]) as bo:
            merge_groups(m, bo, bg["gate"], dilated_groups(m, bo, bg["gate"]))
        with m.buffers(y=[KT, T], sq=[2, T], rstd=[T]) as b:
            project_out(m, bg["gate"], lambda j, k, t: m.evacuate(b["y"], k, j, t))
            layer_norm(m, b["y"], 1, b)


def block2(m):
    with m.buffers(split=("act",), act=[16, T]) as bo:
        pool_gated(m, bo["act"])
        with m.buffers(y=[KT, T], sq=[2, T], rstd=[T]) as b:
            m.pe.after(m.dve.last)
            with m.weight_loop(KT // 2, 2) as i:
                for j in (0, 1):
                    m.open_set(j)
                    s, w = m.take()
                    t = m.project(m.bank[2 * j][:], [w[:, k, :] for k in range(16)], m.tiles(bo["act"], 16), s)
                    m.evacuate(b["y"], i * 2 + j, j, t)
            layer_norm(m, b["y"], 0, b)
    dilated_mixer(m)


def mlstm(m, h, mix):
    a, v, pe = m.act, m.dve, m.pe
    with m.buffers(qk=[4, T], og=[4, T], MV=[TT, 4 * P], ct=[TT, 4]) as b:
        with m.buffers(raw=[2, T + 3], vT=[2, T], lf=[T], z=[T], tmp=[T], one=[T], B=[T], cs=[T], nmu=[T], arg=[T]) as c:
            v.after()
            v.do(v.eng.memset(c["raw"][:], 0.0))
            a.after(v.last)

            def conv(j, k, t):
                raw = c["raw"][:, j, :]
                acc = b["qk"][:, k, :]
                a.after(t)
                t = a.do(a.eng.copy(raw[:, 3:], m.bank[2 * j][:]))
                v.after(t)
                v.do(v.eng.tensor_scalar(acc, raw[:, 0:T], m.col("mlstm_conv_w_3", k), m.col("mlstm_conv_b_3", k), ALU.mult, ALU.add))
                for tap in (1, 2, 3):
                    v.after()
                    v.do(v.eng.scalar_tensor_tensor(acc, raw[:, tap:tap + T], m.col("mlstm_conv_w_3", 4 * tap + k), acc, ALU.mult, ALU.add))
                a.after(v.last)
                t = a.do(a.eng.activation(acc, acc, ACT.Silu))
                v.after(t)
                v.do(v.eng.tensor_scalar(acc, acc, HD ** -0.5 if k < 2 else 1.0, None, ALU.mult), m.freed[j])

            m.pairs(m.tiles(h), 4, conv)

            def value(j, k, t):
                a.after(t)
                t = a.do(a.eng.copy(c["vT"][:, j, :], m.bank[2 * j][:]), m.freed[j])
                pe.after(v.last)
                to_keys(m, c["vT"][:, j, :], b["MV"][:, :, k * P:(k + 1) * P], m.bank[4], t)

            m.pairs(m.tiles(h), 4, value)
            m.pairs(m.tiles(h), 4, lambda j, k, t: (a.after(t), a.do(a.eng.activation(b["og"][:, k, :], m.bank[2 * j][:], ACT.Sigmoid), m.freed[j])))
            s, w = m.take()
            m.open_set(0)
            ti = m.project(m.bank[0][:], [w[:, k, :] for k in range(KT)], m.tiles(h))
            tf = m.project(m.bank[1][:], [w[:, KT + k, :] for k in range(KT)], m.tiles(h), s)
            s, w = m.take()
            m.open_set(1)
            for n in range(TT):
                tw = m.project(m.bank[2][:, 8 * n:8 * n + 8], [x[:, n * P:(n + 1) * P] for x in m.tiles(h)],
                               [w[:, k, 0:8] for k in range(KT)], s if n == TT - 1 else None)
            v.after(tw)
            v.do(v.eng.tensor_scalar(m.iw[:], m.bank[2][:, 0:8 * TT], 8 ** -0.5, None, ALU.mult), m.freed[1])
            r = slice(0, 4)
            for name in ("cs", "nmu", "arg"):
                v.after()
                v.do(v.eng.memset(c[name][:], 0.0))
            v.after()
            v.do(v.eng.memset(c["one"][:], 1.0))
            z, tmp, lf = c["z"][r], c["tmp"][r], c["lf"][r]
            v.after(tf)
            v.do(v.eng.tensor_scalar(z, m.bank[1][r, :], m.col("f_bias_3")[r], None, ALU.add))
            v.after()
            v.do(v.eng.scalar_tensor_tensor(tmp, z, -1.0, z, ALU.mult, ALU.min))
            a.after(v.last)
            t = a.do(a.eng.activation(tmp, tmp, ACT.Exp))
            v.after(t)
            v.do(v.eng.tensor_scalar(tmp, tmp, 1.0, None, ALU.add))
            a.after(v.last)
            t = a.do(a.eng.activation(tmp, tmp, ACT.Ln))
            v.after(t)
            v.do(v.eng.scalar_tensor_tensor(lf, z, 0.0, tmp, ALU.min, ALU.subtract))
            v.after()
            v.do(v.eng.tensor_tensor_scan(c["B"][r], c["one"][r], lf, 0.0, ALU.mult, ALU.add))
            v.after(ti)
            v.do(v.eng.scalar_tensor_tensor(c["cs"][r], m.bank[0][r, :], m.col("i_bias_3")[r], c["B"][r], ALU.add, ALU.subtract), m.freed[0])
            v.after()
            v.do(v.eng.tensor_tensor_scan(tmp, c["one"][r], c["cs"][r], 0.0, ALU.mult, ALU.max))
            v.after()
            v.do(v.eng.tensor_scalar(c["nmu"][r], tmp, -1.0, None, ALU.mult))
            v.after()
            v.do(v.eng.tensor_tensor(c["arg"][r], c["nmu"][r], c["B"][r], ALU.subtract))
            pe.after(v.last)
            for n in range(TT):
                ins = pe.eng.transpose(m.bank[4][:, n * P:(n + 1) * P], c["cs"][:, n * P:(n + 1) * P], m.c("ident"))
            t = pe.do(ins)
            v.after(t)
            v.do(v.eng.tensor_copy(b["ct"][:], m.bank[4][:].rearrange("p (n c) -> p n c", c=P)[:, :, 0:4]))
            m.join()
            mlstm_heads(m, b, c["nmu"], c["arg"], mix)


def mlstm_heads(m, b, nmu, arg, mix):
    a, v, pe = m.act, m.dve, m.pe
    with m.buffers(pick=[4 * P], mub=[T], md=[TT, P], thr=[T], E=[2, T], sc=[2, T], den=[T], hm=[T], sq=[T], rstd=[T]) as c:
        pe.after(m.fetch("pick", c["pick"]))
        for hd in range(4):
            hp = slice(hd % 2 * HD, hd % 2 * HD + HD)
            pick = c["pick"][:, hd * P:(hd + 1) * P]
            t1 = pe.do(m.mm(m.bank[4][:], pick, nmu[:]))
            t2 = pe.do(m.mm(m.bank[5][:], pick, arg[:]))
            a.after(t1)
            t = a.do(a.eng.copy(c["mub"][:], m.bank[4][:]))
            a.after(t2)
            t_thr = a.do(a.eng.activation(c["thr"][:], m.bank[5][:], ACT.Exp))
            v.after(t)
            t_md = v.do(v.eng.tensor_tensor(c["md"][:], c["mub"].rearrange("p (n c) -> p n c", c=P),
                                            m.c("causal_t").unsqueeze(1).broadcast_to([P, TT, P]), ALU.add))
            a.after(t_md)
            used = [None, None]
            pe.after(t_thr)
            for j in range(TT):
                W, e = T - j * P, j % 2
                E, sc = c["E"][:, e, :], c["sc"][:, e, :]
                sb = m.bank[6 + e]
                pe.after(used[e])
                t = pe.do(m.mm(sb[:, 0:W], b["qk"][hp, 2 + hd // 2, j * P:(j + 1) * P], b["qk"][hp, hd // 2, j * P:T]))
                a.after(used[e])
                te = a.do(a.eng.activation(E[:, 0:P], c["md"][:, j, :], ACT.Exp, bias=b["ct"][:, j, hd:hd + 1]))
                if W > P:
                    a.after()
                    te = a.do(a.eng.activation(E[:, P:W], c["mub"][:, (j + 1) * P:T], ACT.Exp, bias=b["ct"][:, j, hd:hd + 1]))
                v.after(t, te, pv if j >= 2 else None)
                used[e] = v.do(v.eng.tensor_tensor(sc[:, 0:W], E[:, 0:W], sb[:, 0:W], ALU.mult))
                pe.after(used[e])
                m.mm(m.bank[4][:, j * P:T], b["MV"][:, j, hd * P:(hd + 1) * P], sc[:, 0:W], j == 0, j == TT - 1)
                pv = pe.do(m.mm(m.bank[5][:, j * P:T], m.c("ones"), sc[:, 0:W], j == 0, j == TT - 1))
            v.after(pv, t_thr)
            v.do(v.eng.scalar_tensor_tensor(c["den"][:], m.bank[5][:], -1.0, c["thr"][:], ALU.mult, ALU.max))
            v.after()
            v.do(v.eng.tensor_tensor(c["den"][:], m.bank[5][:], c["den"][:], ALU.max))
            v.after()
            v.do(v.eng.reciprocal(c["den"][:], c["den"][:]))
            v.after()
            v.do(v.eng.tensor_tensor(c["hm"][:], m.bank[4][:], c["den"][:], ALU.mult))
            a.after(v.last)
            t = a.do(a.eng.activation(c["sq"][:], c["hm"][:], ACT.Square))
            pe.after(t)
            t = pe.do(m.mm(m.bank[5][:], m.c("ones"), c["sq"][:]))
            m.inv_root(c["rstd"][:], m.bank[5][:], t, 1.0 / P, 1e-6)
            v.after()
            v.do(v.eng.scalar_tensor_tensor(c["hm"][:], c["hm"][:], m.col("mlstm_norm_3", hd), c["rstd"][:], ALU.mult, ALU.mult))
            v.after()
            v.do(v.eng.tensor_tensor(mix[:, hd, :], c["hm"][:], b["og"][:, hd, :], ALU.mult))
            m.join()


def select_keys(m, h, sel):
    a, v, pe = m.act, m.dve, m.pe
    with m.buffers(kx=[T], qi=[4, T], sq=[T], rs=[T], rl=[2, T], top=[TT, 8]) as b:
        s, w = m.take()
        m.open_set(0)
        t = m.project(m.bank[0][:], [w[:, k, :] for k in range(KT)], m.tiles(h), s)
        m.evacuate(b["kx"].rearrange("p (o t) -> p o t", o=1), 0, 0, t)
        a.after()
        t = a.do(a.eng.activation(b["sq"][:], b["kx"][:], ACT.Square))
        pe.after(t)
        t = pe.do(m.mm(m.bank[4][:], m.c("headones"), b["sq"][:]))
        m.inv_root(b["rs"][:], m.bank[4][:], t, 1.0 / HD, 1e-6)
        v.after()
        t_k = v.do(v.eng.scalar_tensor_tensor(b["kx"][:], b["kx"][:], m.col("idx_k_norm_3"), b["rs"][:], ALU.mult, ALU.mult))
        m.pairs(m.tiles(h), 4, lambda j, k, t: (a.after(t), a.do(a.eng.mul(b["qi"][:, k, :], m.bank[2 * j][:], HD ** -0.5), m.freed[j])))
        pe.after(a.last, t_k)
        used, read = [None, None], [None, None]
        for n in range(1, TT):
            W = (n + 1) * P
            work = sel[:, n, 0:W]
            for hd in range(8):
                e = hd % 2
                hp = slice(e * HD, e * HD + HD)
                pe.after(used[e])
                t = pe.do(m.mm(m.bank[4 + e][:, 0:W], b["qi"][hp, hd // 2, n * P:W], b["kx"][hp, 0:W]))
                a.after(t, read[e])
                used[e] = a.do(a.eng.activation(b["rl"][:, e, 0:W], m.bank[4 + e][:, 0:W], ACT.Relu))
                v.after(used[e])
                wgt = m.iw[:, 8 * n + hd:8 * n + hd + 1]
                if hd == 0:
                    read[e] = v.do(v.eng.tensor_scalar(work, b["rl"][:, e, 0:W], wgt, 0.0, ALU.mult, ALU.add))
                else:
                    read[e] = v.do(v.eng.scalar_tensor_tensor(work, b["rl"][:, e, 0:W], wgt, work, ALU.mult, ALU.add))
            v.after()
            v.do(v.eng.tensor_tensor(sel[:, n, n * P:W], sel[:, n, n * P:W], m.c("causal"), ALU.add))
        for _ in range(TOPK // 8):
            for n in range(1, TT):
                work = sel[:, n, 0:(n + 1) * P]
                v.after()
                v.do(v.eng.max(b["top"][:, n, :], work))
                v.after()
                v.do(v.eng.match_replace(work, b["top"][:, n, :], work, TAKEN))
        for n in range(1, TT):
            work = sel[:, n, 0:(n + 1) * P]
            v.after()
            v.do(v.eng.tensor_scalar(work, work, 0.5 * TAKEN, NEG, ALU.is_gt, ALU.mult))
        v.after()
        v.do(v.eng.tensor_copy(sel[:, 0, 0:P], m.c("causal")))


def dsa(m, h, mix):
    a, v, pe = m.act, m.dve, m.pe
    line = m.nc.dram_tensor("bias_by_distance", (8, 640), F32, kind="Internal").ap()
    with m.buffers(sel=[TT, T], bias=[8, T]) as bs:
        with m.buffers(rb=[8], bucket=[640], line=[640], skew=[8, T]) as b:
            everyone = [e.last for e in m.compute if e.last]
            t = m.dma(b["rb"][:], m.dram["rel_bias"], everyone, m.act)
            pe.after(t, m.fetch("bucket", b["bucket"]))
            m.mm(m.bank[4][0:8, :], b["rb"][:], b["bucket"][:, 0:T])
            t = pe.do(m.mm(m.bank[5][0:8, 0:P], b["rb"][:], b["bucket"][:, T:T + P]))
            v.after(t)
            v.do(v.eng.tensor_copy(b["line"][0:8, 0:T], m.bank[4][0:8, :]))
            v.after()
            v.do(v.eng.tensor_copy(b["line"][0:8, T:T + P], m.bank[5][0:8, 0:P]))
            t = m.dma(line, b["line"][0:8, :], [v.last], m.act)
            skewed = bass.AP(line.tensor, 0, [[1, P], [640, 8], [1, T]])
            t = m.dma(b["skew"][:], skewed, [t], m.act)
            pe.after(t)
            got = []
            for hd in range(8):
                bank = m.bank[4 + hd % 4]
                pe.after(got[hd - 4] if hd >= 4 else None)
                t = pe.do(m.mm(bank[:], m.c("anti"), b["skew"][:, hd, :]))
                a.after(t)
                got.append(a.do(a.eng.copy(bs["bias"][:, hd, :], bank[:])))
        select_keys(m, h, bs["sel"])
        sel = bs["sel"]
        with m.buffers(q=[T], k=[T], vT=[T], V=[TT, 2 * (HD + 1)], S=[2, T], E=[2, T], PT=[2, T], st=[2, 4], o=[2, P]) as b:
            V = b["V"].rearrange("p k (a c) -> p k a c", a=2)
            v.after()
            v.do(v.eng.memset(b["V"][:], 1.0))
            with m.weight_loop(4, 2) as pair:
                tq, tk, tv = qkv_units(m, h, b["q"], b["k"], b["vT"])
                tV = values_with_ones(m, b, tv)
                pe.after(tq, tk, tV)
                busy = [None, None]
                for i in range(TT):
                    W = (i + 1) * P
                    tok_s, tok_e, tok_p, tok_o = [None] * 2, [None] * 2, [None] * 2, [None] * 2
                    for e in (0, 1):
                        hp = slice(e * HD, e * HD + HD)
                        pe.after(busy[e])
                        tok_s[e] = pe.do(m.mm(m.bank[4 + e][:, 0:W], b["q"][hp, i * P:W], b["k"][hp, 0:W]))
                    for e in (0, 1):
                        S, st = b["S"][:, e, 0:W], b["st"][:, e, :]
                        v.after(tok_s[e])
                        near = bs["bias"][:, bass.ds(pair * 2 + e, 1), T - W:T].rearrange("p o t -> p (o t)")
                        v.do(v.eng.tensor_tensor(S, m.bank[4 + e][:, 0:W], near, ALU.add))
                        v.after()
                        v.do(v.eng.tensor_tensor(S, S, sel[:, i, 0:W], ALU.add))
                        v.after()
                        v.do(v.eng.reduce_max(st[:, 0:1], S, AX))
                        v.after()
                        v.do(v.eng.tensor_scalar(st[:, 1:2], st[:, 0:1], -1.0, None, ALU.mult))
                        a.after(v.last)
                        tok_e[e] = a.do(a.eng.activation(b["E"][:, e, 0:W], S, ACT.Exp, bias=st[:, 1:2]))
                    for e in (0, 1):
                        pe.after(tok_e[e])
                        for k in range(i + 1):
                            ins = pe.eng.transpose(m.bank[6 + e][:, k * P:(k + 1) * P], b["E"][:, e, k * P:(k + 1) * P], m.c("ident"))
                        t = pe.do(ins)
                        a.after(t)
                        tok_p[e] = a.do(a.eng.copy(b["PT"][:, e, 0:W], m.bank[6 + e][:, 0:W]))
                    for e in (0, 1):
                        pe.after(tok_p[e])
                        for k in range(i + 1):
                            ins = m.mm(m.bank[4 + e][:, 0:HD + 1], b["PT"][:, e, k * P:(k + 1) * P], V[:, k, e, :], k == 0, k == i)
                        t = pe.do(ins)
                        v.after(t)
                        v.do(v.eng.reciprocal(b["st"][:, e, 2:3], m.bank[4 + e][:, HD:HD + 1]))
                        v.after()
                        busy[e] = v.do(v.eng.tensor_scalar(b["o"][:, i % 2, e * HD:(e + 1) * HD], m.bank[4 + e][:, 0:HD],
                                                           b["st"][:, e, 2:3], None, ALU.mult))
                    pe.after(busy[1])
                    t = pe.do(pe.eng.transpose(m.bank[6][:, 0:P], b["o"][:, i % 2, :], m.c("ident")))
                    a.after(t)
                    t = a.do(a.eng.copy(tile_of(mix, pair + 4, slice(i * P, W)), m.bank[6][:, 0:P]))
                    pe.after(t)
                m.join()


def block3(m):
    a, v, pe = m.act, m.dve, m.pe
    with m.buffers(mix=[KT, T]) as bm:
        with m.buffers(split=("h",), h=[KT, T], iw=[8 * TT]) as bh:
            m.iw = bh["iw"]
            with m.buffers(sq=[2, T], rstd=[T]) as b:
                m.rms(m.x, bh["h"], "norm_mix_3", b)
            mlstm(m, bh["h"], bm["mix"])
            dsa(m, bh["h"], bm["mix"])

        def add(j, k, t):
            v.after(t)
            v.do(v.eng.tensor_tensor(tile_of(m.x, k), tile_of(m.x, k), m.bank[2 * j][:], ALU.add), m.freed[j])

        project_out(m, bm["mix"], add)
    with m.buffers(split=("act",), act=[FT, T]) as bo:
        with m.buffers(split=("h",), h=[KT, T]) as bh:
            with m.buffers(sq=[2, T], rstd=[T]) as b:
                m.rms(m.x, bh["h"], "norm_ffn_3", b)
            with m.buffers(raw=[2, T + 2], cv=[4, T]) as b:
                v.after()
                v.do(v.eng.memset(b["raw"][:], 0.0))
                a.after(v.last)

                def gate(j, k, tg, tu):
                    for part, t in ((0, tg), (1, tu)):
                        n = 2 * j + part
                        raw, cv = b["raw"][:, j, :], b["cv"][:, n, :]
                        a.after(t, read if part else None)
                        t = a.do(a.eng.copy(raw[:, 2:], m.bank[n][:]))
                        c = k + FT * part
                        v.after(t)
                        v.do(v.eng.tensor_scalar(cv, raw[:, 0:T], m.col("ffn_conv_w_3", c), m.col("ffn_conv_b_3", c), ALU.mult, ALU.add))
                        for tap in (1, 2):
                            v.after()
                            t = v.do(v.eng.scalar_tensor_tensor(cv, raw[:, tap:tap + T], m.col("ffn_conv_w_3", c + 2 * FT * tap), cv, ALU.mult, ALU.add))
                        read = t
                        if part == 0:
                            a.after(t)
                            ts = a.do(a.eng.activation(cv, cv, ACT.Silu))
                    v.after(ts)
                    t = v.do(v.eng.tensor_tensor(b["cv"][:, 2 * j, :], b["cv"][:, 2 * j, :], b["cv"][:, 2 * j + 1, :], ALU.mult))
                    store_split(m, j, b["cv"][:, 2 * j, :], bo["act"], k, t)

                m.gated_pairs(bh["h"], gate)
        with m.buffers(y=[KT, T], sq=[2, T], rstd=[T]) as b:
            m.down(bo["act"], b["y"])
            m.join()
            for k in range(KT):
                v.after()
                v.do(v.eng.tensor_tensor(m.x[:, k, :], m.x[:, k, :], b["y"][:, k, :], ALU.add))
            m.rms(m.x, m.x, "norm_final_3", b)
            m.join()


BLOCKS = (1, 2, 3)


def build(nc, adds_of, arrays_shapes, const_at, plan):
    dram = {k: nc.dram_tensor(f"in_{k}", s, F32, kind="ExternalInput").ap() for k, s in arrays_shapes.items()}
    out = nc.dram_tensor("out_x", (D, T), F32, kind="ExternalOutput").ap()
    m = Machine(nc, adds_of, dram, const_at, plan)
    for n, f in ((1, block1), (2, block2), (3, block3)):
        if n in BLOCKS:
            f(m)
    assert m.taken == len(plan), (m.taken, len(plan))
    m.join()
    done = m.dma(out.rearrange("(k p) t -> p k t", p=P), m.x[:], [e.last for e in m.compute if e.last])
    m.sp.wait(done)
    for s in (0, 1):
        m.sp.wait(m.loaded[s].now())
    return {lp.index: lp.counted for lp in m.seen}


def lay_out(inputs, plan, const):
    flat = {k: np.asarray(v) for k, v in inputs.items()}
    flat["w_grp_a_2"] = flat["w_grp_a_2"].reshape(-1, 512) if "w_grp_a_2" in flat else None
    stream = np.zeros((len(plan) + 1, P, SLOT * P), np.float32)
    for s, slot in enumerate(plan):
        for n, block in enumerate(slot):
            for name, r, nr, c, nc_, part, *to in (block if isinstance(block, list) else [block]):
                a = flat[name]
                a = a[0] if a.ndim == 3 else a
                at = n * P + (to[0] if to else 0)
                stream[s, part:part + nr, at:at + nc_] = a[r:r + nr, c:c + nc_]
    at, n, want = column_plan()
    cols = np.zeros((n, P), np.float32)
    for name, k in want:
        if name in flat:
            a = flat[name].reshape(-1)
            if name == "idx_k_norm_3":
                a = np.concatenate([a, a])
            if k * P == a.size:
                cols[at[name]:at[name] + k] = a.reshape(k, P)
            else:
                full = np.zeros(k * P, np.float32)
                full[:a.size] = a
                cols[at[name]:at[name] + k] = full.reshape(k, P)
    out = {"x": np.ascontiguousarray(flat["x"].reshape(T, D).T), "cols": np.ascontiguousarray(cols.T), "const": const,
           "wstream": stream}
    if "rel_bias_3" in flat:
        out["rel_bias"] = np.zeros((P, 8), np.float32)
        out["rel_bias"][:32] = flat["rel_bias_3"]
    return out


def kernel(**inputs):
    import concourse.bacc as bacc
    from concourse.bass_utils import run_bass_kernel_spmd

    plan = weight_plan(BLOCKS)
    const, const_at = constants()
    arrays = lay_out(inputs, plan, const)
    shapes = {k: a.shape for k, a in arrays.items()}
    adds_of = build(bacc.Bacc("TRN2", target_bir_lowering=False, num_devices=1), {}, shapes, const_at, plan)
    nc = bacc.Bacc("TRN2", target_bir_lowering=False, num_devices=1)
    assert build(nc, adds_of, shapes, const_at, plan) == adds_of
    r = run_bass_kernel_spmd(nc, [{f"in_{k}": a for k, a in arrays.items()}], core_ids=[0])
    return np.ascontiguousarray(r.results[0]["out_x"].T).reshape(1, T, D)
```
